# Optimizing a Trainium2 kernel written in Bass

```python
import math
import jax, jax.numpy as jnp
from jax import lax
import numpy as np

D_MODEL = 1024
BATCH = 1
SEQ = 256
DEPTH = 2

CHUNK = 64
N_MIXERS = 2
N_CONV_LAYERS = (DEPTH + 1) // 2
N_MLA_LAYERS = DEPTH // 2

CONV_WIDTH = 31

MLA_HEADS = 8
MLA_NOPE = 128
MLA_ROPE = 64
MLA_V = 128
MLA_Q_RANK = 384
MLA_KV_RANK = 256
ROPE_THETA = 10000.0
Q_BLOCK = 128

PEER_HEADS = 8
PEER_N_KEYS = 128
PEER_N_EXPERTS = PEER_N_KEYS * PEER_N_KEYS
PEER_D_QUERY = 256
PEER_TOPK = 16
PEER_TOKEN_BLOCK = 128

LN_EPS = 1e-5
RMS_EPS = 1e-6
DEEPNORM_ALPHA = (2 * DEPTH) ** 0.25
DEEPNORM_BETA = (8 * DEPTH) ** -0.25

kernel_name = 'hybrid_conv_mla_peer_deepnorm'

def layer_norm(x, g, b):
    xf = x.astype(jnp.float32)
    mu = jnp.mean(xf, axis=-1, keepdims=True)
    var = jnp.mean(jnp.square(xf - mu), axis=-1, keepdims=True)
    y = (xf - mu) * lax.rsqrt(var + LN_EPS)
    return (y * g.astype(jnp.float32) + b.astype(jnp.float32)).astype(x.dtype)

def rms_norm(x, g):
    xf = x.astype(jnp.float32)
    y = xf * lax.rsqrt(jnp.mean(jnp.square(xf), axis=-1, keepdims=True) + RMS_EPS)
    return (y * g.astype(jnp.float32)).astype(x.dtype)

def rope_tables(positions):
    inv = 1.0 / (ROPE_THETA ** (jnp.arange(0, MLA_ROPE, 2, dtype=jnp.float32) / MLA_ROPE))
    ang = positions.astype(jnp.float32)[..., None] * inv
    return jnp.cos(ang), jnp.sin(ang)

def rotary(t, cos, sin):
    half = t.shape[-1] // 2
    t1, t2 = t[..., :half], t[..., half:]
    cos = cos.astype(t.dtype)
    sin = sin.astype(t.dtype)
    return jnp.concatenate([t1 * cos - t2 * sin, t2 * cos + t1 * sin], axis=-1)

def conv_module(x, w_in, b_in, w_dw, b_dw, ln_g, ln_b, w_out, b_out):
    h = x @ w_in + b_in
    a, gate = jnp.split(h, 2, axis=-1)
    h = a * jax.nn.sigmoid(gate)
    h = lax.conv_general_dilated(
        h, w_dw[:, None, :], window_strides=(1,), padding=[(CONV_WIDTH - 1, 0)],
        dimension_numbers=('NWC', 'WIO', 'NWC'), feature_group_count=D_MODEL) + b_dw
    h = jax.nn.silu(layer_norm(h, ln_g, ln_b))
    return h @ w_out + b_out

def mla_mixer(x, cos, sin, w_in, q_norm, kv_norm, w_uq, w_uk, w_uv, w_out):
    B, S, _ = x.shape
    c = x @ w_in
    c_q = rms_norm(c[..., :MLA_Q_RANK], q_norm)
    c_kv = rms_norm(c[..., MLA_Q_RANK:MLA_Q_RANK + MLA_KV_RANK], kv_norm)
    k_rope = rotary(c[..., MLA_Q_RANK + MLA_KV_RANK:], cos, sin)
    q = (c_q @ w_uq).reshape(B, S, MLA_HEADS, MLA_NOPE + MLA_ROPE)
    q_nope = q[..., :MLA_NOPE]
    q_rope = rotary(q[..., MLA_NOPE:], cos[:, :, None, :], sin[:, :, None, :])
    k_nope = (c_kv @ w_uk).reshape(B, S, MLA_HEADS, MLA_NOPE)
    v = (c_kv @ w_uv).reshape(B, S, MLA_HEADS, MLA_V)
    scale = (MLA_NOPE + MLA_ROPE) ** -0.5
    nb = S // Q_BLOCK
    key_chunk = jnp.arange(S) // CHUNK

    def to_blocks(t):
        return t.reshape(B, nb, Q_BLOCK, *t.shape[2:]).swapaxes(0, 1)

    def attend(args):
        qn, qr, start = args
        s = (jnp.einsum('bqhd,bkhd->bhqk', qn, k_nope)
             + jnp.einsum('bqhr,bkr->bhqk', qr, k_rope)).astype(jnp.float32) * scale
        q_chunk = (start + jnp.arange(Q_BLOCK)) // CHUNK
        mask = key_chunk[None, :] <= q_chunk[:, None]
        s = jnp.where(mask, s, jnp.finfo(jnp.float32).min)
        p = jax.nn.softmax(s, axis=-1).astype(v.dtype)
        return jnp.einsum('bhqk,bkhd->bqhd', p, v)

    starts = jnp.arange(nb, dtype=jnp.int32) * Q_BLOCK
    o = lax.map(attend, (to_blocks(q_nope), to_blocks(q_rope), starts))
    o = o.swapaxes(0, 1).reshape(B, S, MLA_HEADS * MLA_V)
    return o @ w_out

def peer(x, w_q, sub_keys, u, v):
    B, S, D = x.shape
    T = B * S
    xt = x.reshape(T, D)
    q = (xt @ w_q).reshape(T, PEER_HEADS, 2, PEER_D_QUERY // 2)
    s = jnp.einsum('thpd,pnd->thpn', q, sub_keys).astype(jnp.float32)
    sv, si = lax.top_k(s, PEER_TOPK)
    cand = sv[:, :, 0, :, None] + sv[:, :, 1, None, :]
    cv, ci = lax.top_k(cand.reshape(T, PEER_HEADS, PEER_TOPK * PEER_TOPK), PEER_TOPK)
    i1 = jnp.take_along_axis(si[:, :, 0, :], ci // PEER_TOPK, axis=-1)
    i2 = jnp.take_along_axis(si[:, :, 1, :], ci % PEER_TOPK, axis=-1)
    experts = (i1 * PEER_N_KEYS + i2).reshape(T, PEER_HEADS * PEER_TOPK)
    gates = jax.nn.softmax(cv, axis=-1).reshape(T, PEER_HEADS * PEER_TOPK).astype(x.dtype)
    nb = T // PEER_TOKEN_BLOCK

    def expert_block(args):
        xb, eb, gb = args
        ub = jnp.take(u, eb, axis=0)
        a = jax.nn.gelu(jnp.einsum('td,tkd->tk', xb, ub), approximate=False) * gb
        vb = jnp.take(v, eb, axis=0)
        return jnp.einsum('tk,tkd->td', a, vb)

    y = lax.map(expert_block, (xt.reshape(nb, PEER_TOKEN_BLOCK, D),
                               experts.reshape(nb, PEER_TOKEN_BLOCK, -1),
                               gates.reshape(nb, PEER_TOKEN_BLOCK, -1)))
    return y.reshape(B, S, D)

def setup_inputs(seed: int = 0) -> dict:
    key = jax.random.key(seed)
    ks = jax.random.split(key, 32)
    f32 = jnp.float32
    D, L, Lc, Lm = D_MODEL, DEPTH, N_CONV_LAYERS, N_MLA_LAYERS
    nrm = lambda k, shape, s: jax.random.normal(k, shape, f32) * s
    gain = lambda k, shape: 1.0 + 0.02 * jax.random.normal(k, shape, f32)
    x = jax.random.normal(ks[0], (BATCH, SEQ, D), f32)
    offsets = jax.random.randint(ks[1], (BATCH, 1), 0, 4096, dtype=jnp.int32)
    positions = offsets + jnp.arange(SEQ, dtype=jnp.int32)[None, :]
    return {
        'x': x,
        'positions': positions,
        'conv_w_in': nrm(ks[2], (Lc, D, 2 * D), D ** -0.5),
        'conv_b_in': nrm(ks[3], (Lc, 2 * D), 0.02),
        'conv_w_dw': nrm(ks[4], (Lc, CONV_WIDTH, D), CONV_WIDTH ** -0.5),
        'conv_b_dw': nrm(ks[5], (Lc, D), 0.02),
        'conv_ln_g': gain(ks[6], (Lc, D)),
        'conv_ln_b': nrm(ks[7], (Lc, D), 0.02),
        'conv_w_out': nrm(ks[8], (Lc, D, D), D ** -0.5 * DEEPNORM_BETA),
        'conv_b_out': nrm(ks[9], (Lc, D), 0.02),
        'mla_w_in': nrm(ks[10], (Lm, D, MLA_Q_RANK + MLA_KV_RANK + MLA_ROPE), D ** -0.5),
        'mla_q_norm': gain(ks[11], (Lm, MLA_Q_RANK)),
        'mla_kv_norm': gain(ks[12], (Lm, MLA_KV_RANK)),
        'mla_w_uq': nrm(ks[13], (Lm, MLA_Q_RANK, MLA_HEADS * (MLA_NOPE + MLA_ROPE)), MLA_Q_RANK ** -0.5),
        'mla_w_uk': nrm(ks[14], (Lm, MLA_KV_RANK, MLA_HEADS * MLA_NOPE), MLA_KV_RANK ** -0.5),
        'mla_w_uv': nrm(ks[15], (Lm, MLA_KV_RANK, MLA_HEADS * MLA_V), MLA_KV_RANK ** -0.5 * DEEPNORM_BETA),
        'mla_w_out': nrm(ks[16], (Lm, MLA_HEADS * MLA_V, D), (MLA_HEADS * MLA_V) ** -0.5 * DEEPNORM_BETA),
        'peer_w_q': nrm(ks[17], (L, D, PEER_HEADS * PEER_D_QUERY), D ** -0.5),
        'peer_sub_keys': nrm(ks[18], (L, 2, PEER_N_KEYS, PEER_D_QUERY // 2), (PEER_D_QUERY // 2) ** -0.5),
        'peer_u': nrm(ks[19], (L, PEER_N_EXPERTS, D), D ** -0.5),
        'peer_v': nrm(ks[20], (L, PEER_N_EXPERTS, D), DEEPNORM_BETA),
        'ln1_g': gain(ks[21], (L, D)),
        'ln1_b': nrm(ks[22], (L, D), 0.02),
        'ln2_g': gain(ks[23], (L, D)),
        'ln2_b': nrm(ks[24], (L, D), 0.02),
    }

def reference(x, positions, conv_w_in, conv_b_in, conv_w_dw, conv_b_dw, conv_ln_g, conv_ln_b,
              conv_w_out, conv_b_out, mla_w_in, mla_q_norm, mla_kv_norm, mla_w_uq, mla_w_uk,
              mla_w_uv, mla_w_out, peer_w_q, peer_sub_keys, peer_u, peer_v,
              ln1_g, ln1_b, ln2_g, ln2_b):
    cos, sin = rope_tables(positions)
    for i in range(DEPTH):
        j = i // N_MIXERS
        if i % N_MIXERS == 0:
            mix = conv_module(x, conv_w_in[j], conv_b_in[j], conv_w_dw[j], conv_b_dw[j],
                              conv_ln_g[j], conv_ln_b[j], conv_w_out[j], conv_b_out[j])
        else:
            mix = mla_mixer(x, cos, sin, mla_w_in[j], mla_q_norm[j], mla_kv_norm[j],
                            mla_w_uq[j], mla_w_uk[j], mla_w_uv[j], mla_w_out[j])
        x = layer_norm(DEEPNORM_ALPHA * x + mix, ln1_g[i], ln1_b[i])
        ff = peer(x, peer_w_q[i], peer_sub_keys[i], peer_u[i], peer_v[i])
        x = layer_norm(DEEPNORM_ALPHA * x + ff, ln2_g[i], ln2_b[i])
    return x


_drawn_inputs = setup_inputs


def setup_inputs(seed=0):
    import zlib

    import numpy as np

    out = dict(_drawn_inputs(seed))
    spreads = {}
    factors = {'mla_q_norm': 8.0, 'mla_kv_norm': 8.0}
    for name, (base, spread) in spreads.items():
        noise = np.random.default_rng([zlib.crc32(name.encode()), seed]).standard_normal(out[name].shape)
        drawn = base * np.exp(spread * noise) if base else spread * noise
        out[name] = __import__('jax').numpy.asarray(drawn.astype(out[name].dtype))
    for name, factor in factors.items():
        out[name] = (out[name] * factor).astype(out[name].dtype)
    return out
```

```python
from contextlib import ExitStack

import concourse.bass as bass
from concourse import mybir

F32 = mybir.dt.float32
F32R = mybir.dt.float32r
I32 = mybir.dt.int32
U32 = mybir.dt.uint32
ACT = mybir.ActivationFunctionType
ALU = mybir.AluOpType
AX = mybir.AxisListType

P = 128
D = 1024
T = 256
HALVES = T // P
KD = D // P
DEPTH = 2
ALPHA = float((2 * DEPTH) ** 0.25)
LN_EPS = 1e-5
RMS_EPS = 1e-6

TAPS = 31
PAD = TAPS - 1
ROW = PAD + T + 2

HEADS = 8
NOPE, ROPE = 128, 64
Q_RANK, KV_RANK = 384, 256
KQ, KKV = Q_RANK // P, KV_RANK // P
CHUNK = 64
SCALE = float((NOPE + ROPE) ** -0.5)
MASKED = -1e30

PH = 8
NKEYS = 128
TOPK = 16
HP = 2 * PH
LOWEST = -3.0e38

RING = 3
GROUP = 4
GROUPS = T // GROUP
POOL_U = 45

STREAM = [("conv_in", 2 * KD), ("conv_out", KD), ("wq0", HP), ("u0", NKEYS), ("v0", NKEYS),
          ("mla_in", KQ + KKV + 2), ("mla_out", KD), ("wq1", HP), ("u1", NKEYS), ("v1", NKEYS)]
FIRST, BLOCKS = {}, {}
_g = 0
for _name, _n in STREAM:
    FIRST[_name], BLOCKS[_name] = _g, _n
    _g += _n
TOTAL = _g

LOW_BY = []
_cuts = [(0, "pool"), (FIRST["conv_out"] + RING, "vector")]
for _l in range(DEPTH):
    _cuts += [(FIRST[f"u{_l}"] + RING, "pool"), (FIRST[f"u{_l}"] + RING + POOL_U, "vector")]
    if _l == 0:
        _cuts += [(FIRST["mla_in"] + RING, "pool"), (FIRST["mla_out"] + RING, "vector")]
_made = {"pool": 0, "vector": 0}
for _i, (_a, _who) in enumerate(_cuts):
    _b = _cuts[_i + 1][0] if _i + 1 < len(_cuts) else TOTAL
    LOW_BY.append((_a, _b, _who, _made[_who]))
    _made[_who] += _b - _a

PROJECTED = {"conv_in": 0, "wq0": 2 * KD, "u0": 2 * KD + HP, "mla_in": 2 * KD + HP + NKEYS}
PROJECTED["wq1"] = PROJECTED["mla_in"] + BLOCKS["mla_in"]
PROJECTED["u1"] = PROJECTED["wq1"] + HP

C_BIN, C_BDW, C_LNG, C_LNB, C_TAPS = 0, 2 * KD, 3 * KD, 4 * KD, 5 * KD
CONV_COLS = 5 * KD + KD * TAPS
M_QN, M_KVN, M_FREQ = 0, KQ, KQ + KKV
MLA_COLS = KQ + KKV + 1
LN_ROWS = [3, 2, 2, 2]


def low_parts(a, b):
    for lo, hi, who, made in LOW_BY:
        if max(a, lo) < min(b, hi):
            yield max(a, lo), min(b, hi), who, made - lo


def in_threes(eng, a, b, body):
    rounds = (b - a) // RING
    if rounds >= 2:
        with eng.Fori(0, rounds) as i:
            for r in range(RING):
                body(i, a + r)
        a += RING * rounds
    for g in range(a, b):
        body(0, g)


def program(nc, x_rows, x_cols, positions, conv_par, mla_par, ln_par, keys, w_uq, w_uk, w_uv,
            blocks, out):
    with ExitStack() as ctx:
        def sb(name, shape, dtype=F32):
            return ctx.enter_context(nc.sbuf_tensor(name, shape, dtype))

        def sem(name):
            return ctx.enter_context(nc.semaphore(name))

        big = sb("big", [P, NKEYS, T])
        raw = sb("raw", [P, RING, D])
        high = sb("high", [P, RING, D], F32R)
        low = sb("low", [P, RING, D], F32R)
        xT_high = sb("xT_high", [P, KD, T], F32R)
        xT_low = sb("xT_low", [P, KD, T], F32R)
        x = sb("x", [P, HALVES, D])
        aux = sb("aux", [P, 3 * D])
        iota = sb("iota", [P, P])
        ident = sb("ident", [P, P])
        ones = sb("ones", [P, P])
        chosenT = sb("chosenT", [P, 3, T])
        keysT = sb("keysT", [P, 2, NKEYS])
        stats = sb("stats", [P, 64])

        work = ctx.enter_context(nc.psum_tensor("work", [P, 4, 512], F32))
        y = ctx.enter_context(nc.psum_tensor("y", [P, 4, 512], F32))

        def room(slot, width, dtype=None):
            flat = big[:].rearrange("p b t -> p (b t)")[:, slot * T:slot * T + width]
            return flat if dtype is None else flat.bitcast(dtype)

        xT_in = room(0, KD * T)
        conv_p = room(8, CONV_COLS)
        value_buf = room(10, 2 * T).rearrange("p (s t) -> p s t", s=2)
        gate_buf = room(12, 2 * T).rearrange("p (s t) -> p s t", s=2)
        padded = room(14, KD * ROW).rearrange("p (k t) -> p k t", k=KD)
        conv = room(24, KD * T).rearrange("p (k t) -> p k t", k=KD)
        squares = room(32, KD * T).rearrange("p (k t) -> p k t", k=KD)
        mean_c, var_c, std_c, rstd_c = (room(40 + n, T) for n in range(4))

        queryT = room(112, HP * T).rearrange("p (j t) -> p j t", j=HP)
        scores = room(96, HALVES * HP * NKEYS).rearrange("p (j n) -> p j n", n=NKEYS)
        top_v = room(80, HALVES * HP * TOPK)
        top_i = room(82, HALVES * HP * TOPK)
        cand_v = room(84, HALVES * PH * TOPK)
        cand_i = room(85, HALVES * PH * TOPK, U32)
        rank1_u, rank2_u = room(86, T, U32), room(87, T, U32)
        rank1, rank2 = room(88, T), room(89, T)
        sel_v = room(90, TOPK)
        sel_i = room(91, TOPK, U32)
        row_a, row_b = room(92, T), room(93, T)
        gate_sum = room(94, HALVES * PH)
        gate_inv = room(95, HALVES * PH)
        match = room(96, PH * TOPK * TOPK)
        picked = room(104, PH * TOPK * TOPK)
        onehot2 = aux[:, 0:8 * P].rearrange("p (s n) -> p s n", n=P)
        onehot1 = aux[:, 8 * P:16 * P].rearrange("p (s n) -> p s n", n=P)
        chosen = aux[:, 16 * P:16 * P + 3 * T].rearrange("p (q t) -> p q t", q=3)

        latent = room(0, (KQ + KKV) * T).rearrange("p (k t) -> p k t", t=T)
        k_rot = room(5, 2 * T).rearrange("p (s t) -> p s t", s=2)
        lat_sq = room(7, (KQ + KKV) * T).rearrange("p (k t) -> p k t", t=T)
        pos_i = room(12, T, I32)
        angle, turns, turns_hi, turns_lo = (room(13 + n, T) for n in range(4))
        spare = room(17, T)
        cosT, sinT = room(18, T), room(19, T)
        rms = room(20, 2 * T).rearrange("p (s t) -> p s t", s=2)
        latent_n = room(22, (KQ + KKV) * T).rearrange("p (k t) -> p k t", t=T)
        k_turned = room(27, 2 * T).rearrange("p (s t) -> p s t", s=2)
        mla_p = room(29, MLA_COLS)
        mask = room(30, 3 * P)
        queries = room(32, 12 * T).rearrange("p (j t) -> p j t", t=T)
        q_turned = room(44, 4 * T).rearrange("p (j t) -> p j t", t=T)
        turn_tmp = room(48, 2 * T).rearrange("p (s t) -> p s t", s=2)
        keys_n = room(50, HEADS * T).rearrange("p (j t) -> p j t", t=T)
        values = room(58, HALVES * D).rearrange("p (h n) -> p h n", n=D)
        probs = room(66, 2 * 3 * P).rearrange("p (s n) -> p s n", s=2)
        probsT = room(69, 2 * 3 * P).rearrange("p (s n) -> p s n", s=2)
        att_st = room(72, 64)
        uq_w = room(74, 12 * KQ * P).rearrange("p (j k c) -> p j k c", k=KQ, c=P)
        uk_w = room(92, HEADS * KKV * P).rearrange("p (j k c) -> p j k c", k=KKV, c=P)
        uv_w = room(100, KKV * D).rearrange("p (k n) -> p k n", n=D)
        k_masked = room(108, 4 * 2 * T).rearrange("p (q s t) -> p q s t", q=4, s=2)

        landed = [sem(f"block_landed_{s}") for s in range(RING)]
        high_made = sem("high_made")
        low_made = {"pool": sem("low_made_by_pool"), "vector": sem("low_made_by_vector")}
        block_used = sem("block_used")
        emptied = sem("emptied")
        inputs_in = sem("inputs_in")
        keys_in = sem("keys_in")
        x_in = sem("x_in")
        ln_in = [sem(f"ln_rows_in_{n}") for n in range(2 * DEPTH)]
        mla_in = sem("mla_weights_in")
        consts = sem("constants_made")
        pool_fill = sem("pool_fill")
        a_high = sem("a_high_made")
        a_low = sem("a_low_made")
        x_ready = sem("x_normalised")
        x_turned = sem("x_transposed")
        xT_hi_ok = sem("xT_high_made")
        xT_lo_ok = sem("xT_low_made")
        var_ok = sem("variance_made")
        std_ok = sem("std_made")
        v_step = sem("vector_step")
        v_loop = sem("vector_loop_step")
        a_step = sem("scalar_step")
        glu_ok = sem("glu_made")
        conv_done = sem("conv_done")
        stat_mm = sem("column_sums_made")
        mean_ok = sem("centred")
        sq_ok = sem("squares_made")
        cvar_ok = sem("conv_variance_made")
        cstd_ok = sem("conv_std_made")
        norm_ok = sem("conv_normalised")
        silu_ok = sem("silu_made")
        score_mm = sem("scores_made")
        score_ok = sem("scores_copied")
        expo_in = sem("gates_centred")
        expo_ok = sem("gates_exponentiated")
        chosen_ok = sem("experts_chosen")
        chosen_mm = sem("chosen_transposed")
        chosenT_ok = sem("chosen_copied")
        index_ok = sem("group_indices_copied")
        hot1_ok = sem("onehot1_made")
        hot2_ok = sem("onehot2_made")
        spread_ok = sem("gates_spread")
        gated = sem("hidden_gated")
        lat_sq_ok = sem("latent_squares")
        rms_mm = sem("rms_sums")
        rms_var = sem("rms_variance")
        rms_std = sem("rms_std")
        lat_ok = sem("latent_normalised")
        ang_ok = sem("angles_made")
        trig_ok = sem("sines_made")
        small_mm = sem("small_projection")
        small_ok = sem("small_emptied")
        value_mm = sem("values_made")
        value_ok = sem("values_copied")
        q_turn_ok = sem("queries_turned")
        att_s = sem("attention_scores")
        att_m = sem("attention_max")
        att_e = sem("attention_exp")
        att_p = sem("attention_probs")
        att_t = sem("attention_transposed")
        att_c = sem("attention_probsT")
        att_o = sem("attention_out")
        att_h = sem("attention_out_high")
        att_l = sem("attention_out_low")
        out_ok = sem("output_stored")
        waits_taken = sem("waits_taken")

        def g_of(i, c):
            return i * RING + c

        def wait_apart(eng, semaphore, value):
            eng.wait_ge(semaphore, value)
            if not isinstance(value, int):
                eng.sem_inc(waits_taken, 1)

        end_of = {name: FIRST[name] + BLOCKS[name] for name in FIRST}
        block = ctx.enter_context(nc.Block())

        @block.sync
        def _(sp):
            sp.dma_start(xT_in.rearrange("p (k t) -> p k t", k=KD), x_cols).then_inc(inputs_in, 16)
            sp.dma_start(conv_p, conv_par).then_inc(inputs_in, 16)

            def load(name, i, c):
                slot = c % RING
                src = blocks[name[:-1] if name[-1] in "01" else name]
                at = i * RING + (c - FIRST[name])
                if name[-1] in "01":
                    src = src[int(name[-1])]
                sp.dma_start(raw[:, slot, :],
                             src[bass.ds(at, 1)].rearrange("o p c -> p (o c)")).then_inc(landed[slot], 16)

            for g in range(RING):
                load("conv_in", 0, g)
            for name, _ in STREAM:
                a = max(FIRST[name], RING)
                for lo, hi, who, offset in low_parts(a - RING, end_of[name] - RING):
                    def one(i, c):
                        wait_apart(sp, high_made, g_of(i, c - RING + 1))
                        wait_apart(sp, low_made[who], g_of(i, c - RING + 1 + offset))
                        load(name, i, c)
                    in_threes(sp, lo + RING, hi + RING, one)
            for h in range(HALVES):
                sp.wait_ge(x_ready, 2 * (2 * DEPTH - 1) + h + 1)
                sp.dma_start(out[h], x[:, h, :]).then_inc(out_ok, 16)
            sp.wait_ge(out_ok, 16 * HALVES)

        def make_low(eng, ops, who, i, c):
            slot = c % RING
            eng.wait_ge(high_made, g_of(i, c + 1))
            ops.tensor_tensor(low[:, slot, :], raw[:, slot, :], high[:, slot, :].bitcast(F32),
                              ALU.subtract).then_inc(low_made[who], 1)

        @block.gpsimd
        def _(pool):
            def low_stage(name_from, a, b):
                in_threes(pool, a, b, lambda i, c: make_low(pool, nc.gpsimd, "pool", i, c))

            nc.gpsimd.iota(iota[:], [[1, P]], base=0, channel_multiplier=0,
                           allow_small_or_imprecise_dtypes=True).then_inc(consts, 1)
            nc.gpsimd.memset(ident[:], 0.0).then_inc(pool_fill, 1)
            nc.gpsimd.memset(ones[:], 1.0).then_inc(consts, 1)
            nc.gpsimd.memset(padded[:, :, 0:PAD], 0.0).then_inc(consts, 1)
            pool.wait_ge(pool_fill, 1)
            nc.gpsimd.affine_select(out=ident[:], in_=ident[:], compare_op=ALU.not_equal, fill=1.0,
                                    base=0, pattern=[[-1, P]], channel_multiplier=1).then_inc(consts, 1)
            low_stage("conv_in", 0, FIRST["conv_out"] + RING)
            for layer in range(DEPTH):
                u0 = FIRST[f"u{layer}"] + RING
                low_stage("u", u0, u0 + POOL_U)
                pool.wait_ge(chosenT_ok, layer + 1)

                def hot1(i, q, peeled=False):
                    n = layer * GROUPS
                    if not peeled:
                        pool.wait_ge(spread_ok, i + (n + q - 1))
                    s = (q % 2) * GROUP
                    idx = stats[:, 40 + s:40 + s + GROUP]
                    nc.gpsimd.tensor_copy(idx, chosenT[:, 0, bass.ds(i * GROUP + q * GROUP, GROUP)]
                                          ).then_inc(index_ok, 1)
                    wait_apart(pool, index_ok, i + (n + q + 1))
                    for t in range(GROUP):
                        last = nc.gpsimd.tensor_scalar(onehot1[:, s + t, :], iota[:], idx[:, t:t + 1],
                                                       None, ALU.is_equal)
                    last.then_inc(hot1_ok, 1)
                hot1(0, 0, True)
                hot1(0, 1, True)
                with pool.Fori(0, GROUPS // 2 - 1) as i:
                    for q in range(2):
                        hot1(i * 2, q + 2)
                if layer == 0:
                    pool.wait_ge(block_used, end_of["v0"])
                    nc.gpsimd.memset(mask, 0.0).then_inc(pool_fill, 1)
                    nc.gpsimd.memset(room(108, 4 * 2 * T), 0.0).then_inc(consts, 1)
                    pool.wait_ge(pool_fill, 2)
                    nc.gpsimd.memset(mask[0:CHUNK, CHUNK:P], MASKED).then_inc(consts, 1)
                    nc.gpsimd.memset(mask[0:CHUNK, 3 * P - CHUNK:3 * P], MASKED).then_inc(consts, 1)
                    low_stage("mla_in", FIRST["mla_in"] + RING, FIRST["mla_out"] + RING)

        @block.tensor
        def _(pe):
            def wait_low(who, offset, i, c):
                pe.wait_ge(low_made[who], g_of(i, c + 1 + offset))

            def project(name):
                first = FIRST[name]
                for lo, hi, who, offset in low_parts(first, end_of[name]):
                    def one(i, c):
                        wait_low(who, offset, i, c)
                        if not (c < first + RING):
                            pe.wait_ge(emptied, g_of(i, c - RING + 1 - first + PROJECTED[name]))
                        s = c % RING
                        for k in range(KD):
                            cols = slice(k * P, (k + 1) * P)
                            for n, (w, m) in enumerate(((high, xT_high), (high, xT_low), (low, xT_high))):
                                mm = nc.tensor.matmul(work[:, s, 0:T], w[:, s, cols], m[:, k, :],
                                                      start=(k == 0 and n == 0),
                                                      stop=(k == KD - 1 and n == 2))
                        mm.then_inc(block_used, 1)
                    head = min(hi, first + RING)
                    for g in range(lo, head):
                        one(0, g)
                    in_threes(pe, max(lo, head), hi, one)

            def combine_block(a_slot, s, start, stop):
                for h in range(HALVES):
                    rows = slice(h * P, (h + 1) * P)
                    for n, (a, v) in enumerate(((xT_high, high), (xT_high, low), (xT_low, high))):
                        for m in range(2):
                            mm = nc.tensor.matmul(y[:, 2 * h + m, :], a[:, a_slot, rows],
                                                  v[:, s, m * 512:(m + 1) * 512],
                                                  start=(start and n == 0), stop=(stop and n == 2))
                mm.then_inc(block_used, 1)

            def combine_all(name):
                for lo, hi, who, offset in low_parts(FIRST[name], end_of[name]):
                    for g in range(lo, hi):
                        wait_low(who, offset, 0, g)
                        t = g - FIRST[name]
                        combine_block(t, g % RING, t == 0, t == KD - 1)

            def column_sums(bank, col, src, chunks):
                for n, k in enumerate(chunks):
                    mm = nc.tensor.matmul(work[:, bank, col:col + T], ones[:], src[:, k, :],
                                          start=(n == 0), stop=(n == len(chunks) - 1))
                return mm

            def turn_x(n):
                for h in range(HALVES):
                    pe.wait_ge(x_ready, HALVES * n + h + 1)
                    for k in range(KD):
                        mm = nc.tensor.transpose(work[:, 2 * h + k // 4, (k % 4) * P:(k % 4 + 1) * P],
                                                 x[:, h, k * P:(k + 1) * P], ident[:])
                    mm.then_inc(x_turned, 1)

            def wait_xT(n):
                pe.wait_ge(xT_hi_ok, n)
                pe.wait_ge(xT_lo_ok, n)

            wait_xT(1)
            project("conv_in")
            pe.wait_ge(consts, 4)
            pe.wait_ge(conv_done, 1)
            column_sums(3, 0, conv, range(KD)).then_inc(stat_mm, 1)
            pe.wait_ge(sq_ok, 1)
            pe.wait_ge(mean_ok, 1)
            column_sums(3, T, squares, range(KD)).then_inc(stat_mm, 1)
            wait_xT(2)
            combine_all("conv_out")

            for layer in range(DEPTH):
                if layer == 1:
                    wait_xT(6)
                    project("mla_in")
                    pe.wait_ge(lat_sq_ok, 1)
                    column_sums(3, 0, lat_sq, range(KQ))
                    column_sums(3, T, lat_sq, range(KQ, KQ + KKV)).then_inc(rms_mm, 1)
                    pe.wait_ge(lat_ok, 1)
                    pe.wait_ge(mla_in, 16 * 5)
                    done = 0
                    for j in range(12 + HEADS):
                        if j >= 4:
                            pe.wait_ge(small_ok, j - 3)
                        elif j < 3:
                            pe.wait_ge(emptied, PROJECTED["wq1"])
                        w, chunks, k0 = (uq_w[:, j], KQ, 0) if j < 12 else (uk_w[:, j - 12], KKV, KQ)
                        for k in range(chunks):
                            mm = nc.tensor.matmul(work[:, j % 4, 0:T], w[:, k, :], latent_n[:, k0 + k, :],
                                                  start=(k == 0), stop=(k == chunks - 1))
                        mm.then_inc(small_mm, 1)
                    for h in range(HALVES):
                        for m in range(2):
                            for k in range(KKV):
                                mm = nc.tensor.matmul(y[:, 2 * h + m, :],
                                                      latent_n[:, KQ + k, h * P:(h + 1) * P],
                                                      uv_w[:, k, m * 512:(m + 1) * 512],
                                                      start=(k == 0), stop=(k == KKV - 1))
                        mm.then_inc(value_mm, 1)

                    def att_scores(h):
                        if h >= 2:
                            pe.wait_ge(att_m, h - 1)
                        for q in range(HALVES):
                            n = (q + 1) * P
                            cols = slice(q * P, q * P + n)
                            rows = slice(q * P, (q + 1) * P)
                            nc.tensor.matmul(work[:, h % 2, cols], queries[:, 4 + h, rows],
                                             keys_n[:, h, 0:n], start=True, stop=False)
                            for s in range(2):
                                mm = nc.tensor.matmul(work[:, h % 2, cols],
                                                      q_turned[:, 2 * (h // 4) + s, rows],
                                                      k_masked[:, h % 4, s, 0:n],
                                                      start=False, stop=(s == 1))
                        mm.then_inc(att_s, 1)

                    def att_out(h):
                        pe.wait_ge(att_p, h + 1)
                        if h >= 1:
                            pe.wait_ge(att_c, h)
                        for q in range(3):
                            mm = nc.tensor.transpose(work[:, 2, q * P:(q + 1) * P],
                                                     probs[:, h % 2, q * P:(q + 1) * P], ident[:])
                        mm.then_inc(att_t, 1)

                    def att_mix(h):
                        pe.wait_ge(att_c, h + 1)
                        if h >= 2:
                            pe.wait_ge(att_l, h - 1)
                        for q, key, start, stop in ((0, 0, True, True), (1, 0, True, False), (1, 1, False, True)):
                            mm = nc.tensor.matmul(y[:, h % 2, q * P:(q + 1) * P],
                                                  values[:, key, h * P:(h + 1) * P],
                                                  probsT[:, h % 2, (q + key) * P:(q + key + 1) * P],
                                                  start=start, stop=stop)
                        mm.then_inc(att_o, 1)

                    pe.wait_ge(small_ok, 12 + HEADS)
                    pe.wait_ge(q_turn_ok, 1)
                    pe.wait_ge(value_ok, 2)
                    att_scores(0)
                    att_scores(1)
                    for h in range(HEADS):
                        att_out(h)
                        if h + 2 < HEADS:
                            att_scores(h + 2)
                        att_mix(h)
                    pe.wait_ge(att_h, HEADS)
                    pe.wait_ge(att_l, HEADS)
                    combine_all("mla_out")

                turn_x(2 * layer)
                wait_xT((4, 8)[layer])
                project(f"wq{layer}")
                pe.wait_ge(emptied, PROJECTED[f"wq{layer}"] + HP)
                pe.wait_ge(keys_in, 16 * (layer + 1))
                for h in range(HALVES):
                    for j in range(HP):
                        if j % 4 == 0 and h == 1:
                            pe.wait_ge(score_ok, 8 * layer + j // 4 + 1)
                        mm = nc.tensor.matmul(y[:, j // 4, (j % 4) * P:(j % 4 + 1) * P],
                                              queryT[:, j, h * P:(h + 1) * P], keysT[:, j % 2, :],
                                              start=True, stop=True)
                        if j % 4 == 3:
                            mm.then_inc(score_mm, 1)
                project(f"u{layer}")
                pe.wait_ge(chosen_ok, layer + 1)
                for q in range(3):
                    for h in range(HALVES):
                        n = 2 * q + h
                        mm = nc.tensor.transpose(y[:, n // 4, (n % 4) * P:(n % 4 + 1) * P],
                                                 chosen[:, q, h * P:(h + 1) * P], ident[:])
                mm.then_inc(chosen_mm, 1)
                pe.wait_ge(emptied, PROJECTED[f"u{layer}"] + NKEYS)

                def spread(i, q, peeled=False):
                    n = layer * GROUPS
                    pe.wait_ge(hot1_ok, i + (n + q + 1))
                    pe.wait_ge(hot2_ok, i + (n + q + 1))
                    if not peeled:
                        pe.wait_ge(gated, i + (n + q - 3))
                    s = (q % 2) * GROUP
                    for t in range(GROUP):
                        mm = nc.tensor.matmul(work[:, q % 4, t * P:(t + 1) * P], onehot2[:, s + t, :],
                                              onehot1[:, s + t, :], start=True, stop=True)
                    mm.then_inc(spread_ok, 1)
                for q in range(4):
                    spread(0, q, True)
                with pe.Fori(0, GROUPS // 4 - 1) as i:
                    for q in range(4):
                        spread(i * 4, q + 4)

                v = f"v{layer}"
                first = FIRST[v]

                def gathered(start, stop, who, offset, i, c):
                    wait_low(who, offset, i, c)
                    pe.wait_ge(a_low, g_of(i, c + 1 - first + NKEYS * layer))
                    combine_block(c % RING, c % RING, start, stop)
                for lo, hi, who, offset in low_parts(first, end_of[v]):
                    if lo == first:
                        gathered(True, False, who, offset, 0, first)
                        lo += 1
                    last = hi == end_of[v]
                    in_threes(pe, lo, hi - last, lambda i, c: gathered(False, False, who, offset, i, c))
                    if last:
                        gathered(False, True, who, offset, 0, hi - 1)
                if layer + 1 < DEPTH:
                    turn_x(2 * layer + 1)

        @block.scalar
        def _(act):
            A = nc.scalar.activation

            def make_high(i, c):
                slot = c % RING
                act.wait_ge(landed[slot], i * 16 + 16 * (c // RING + 1))
                if c >= RING:
                    act.wait_ge(block_used, g_of(i, c - RING + 1))
                A(high[:, slot, :], raw[:, slot, :], ACT.Copy).then_inc(high_made, 1)

            def project(name, empty, first=0):
                g0 = FIRST[name]

                def one(i, c):
                    act.wait_ge(block_used, g_of(i, c + 1))
                    empty(i, c - g0, c % RING)
                    if c + RING < TOTAL:
                        make_high(i, c + RING)
                in_threes(act, g0 + first, end_of[name], one)

            def ln_rows(n):
                for r in range(LN_ROWS[n]):
                    act.dma_start(aux[:, r * D:(r + 1) * D],
                                  ln_par[n, r:r + 1, :].to_broadcast([P, D])).then_inc(ln_in[n], 16)

            def std(n):
                act.wait_ge(var_ok, n + 1)
                A(stats[:, 30:32], stats[:, 28:30], ACT.Sqrt).then_inc(std_ok, 1)

            def split_xT(n):
                for h in range(HALVES):
                    act.wait_ge(x_turned, HALVES * n + h + 1)
                    A(xT_high[:, :, h * P:(h + 1) * P],
                      work[:, 2 * h:2 * h + 2, :].rearrange("p b (k t) -> p (b k) t", t=P),
                      ACT.Copy).then_inc(xT_hi_ok, 1)

            for h in range(HALVES):
                act.dma_start(x[:, h, :], x_rows[h]).then_inc(x_in, 16)
            ln_rows(0)
            act.wait_ge(inputs_in, 16 * 2)
            A(xT_high[:], xT_in.rearrange("p (k t) -> p k t", k=KD), ACT.Copy).then_inc(xT_hi_ok, 1)
            for g in range(RING):
                make_high(0, g)
            act.dma_start(keysT[:], keys[0]).then_inc(keys_in, 16)

            for t in range(2 * KD):
                act.wait_ge(block_used, t + 1)
                chunk, gate = t // 2, t % 2
                bias = conv_p[:, C_BIN + gate * KD + chunk:C_BIN + gate * KD + chunk + 1]
                if chunk >= 2 and not gate:
                    act.wait_ge(glu_ok, chunk - 1)
                dst = gate_buf if gate else value_buf
                A(dst[:, chunk % 2, :], work[:, t % RING, 0:T], ACT.Sigmoid if gate else ACT.Identity,
                  bias=bias).then_inc(emptied, 1)
                make_high(0, t + RING)
            act.wait_ge(mean_ok, 1)
            A(squares[:], conv[:], ACT.Square).then_inc(sq_ok, 1)
            act.wait_ge(cvar_ok, 1)
            A(std_c, var_c, ACT.Sqrt).then_inc(cstd_ok, 1)
            act.wait_ge(norm_ok, 1)
            for k in range(KD):
                last = A(squares[:, k, :], conv[:, k, :], ACT.Silu,
                         bias=conv_p[:, C_LNB + k:C_LNB + k + 1],
                         scale=conv_p[:, C_LNG + k:C_LNG + k + 1])
            last.then_inc(silu_ok, 1)
            act.wait_ge(silu_ok, 1)
            A(xT_high[:], squares[:], ACT.Copy).then_inc(xT_hi_ok, 1)
            in_threes(act, FIRST["conv_out"], end_of["conv_out"], lambda i, c: make_high(i, c + RING))

            for layer in range(DEPTH):
                if layer == 1:
                    act.wait_ge(block_used, end_of["v0"])
                    for dst, src in ((mla_p, mla_par), (uq_w, w_uq), (uk_w, w_uk), (uv_w, w_uv)):
                        act.dma_start(dst, src).then_inc(mla_in, 16)
                    act.dma_start(keysT[:], keys[1]).then_inc(keys_in, 16)
                    act.dma_start(pos_i, positions.to_broadcast([P, T])).then_inc(mla_in, 16)
                    act.wait_ge(x_ready, HALVES * 2)
                    ln_rows(2)
                    split_xT(1)

                    def empty(i, t, bank):
                        dst = latent[:, t, :] if t < KQ + KKV else k_rot[:, t - KQ - KKV, :]
                        A(dst, work[:, bank, 0:T], ACT.Copy).then_inc(emptied, 1)
                    g0 = FIRST["mla_in"]
                    for t in range(BLOCKS["mla_in"]):
                        act.wait_ge(block_used, g0 + t + 1)
                        empty(0, t, (g0 + t) % RING)
                        make_high(0, g0 + t + RING)
                    act.wait_ge(emptied, PROJECTED["wq1"])
                    A(lat_sq[:], latent[:], ACT.Square).then_inc(lat_sq_ok, 1)
                    act.wait_ge(rms_var, 1)
                    A(rms[:], rms[:], ACT.Sqrt).then_inc(rms_std, 1)
                    act.wait_ge(ang_ok, 1)
                    A(sinT, angle, ACT.Sin)
                    A(cosT, turns, ACT.Sin).then_inc(trig_ok, 1)
                    for j in range(12 + HEADS):
                        act.wait_ge(small_mm, j + 1)
                        dst = queries[:, j, :] if j < 12 else keys_n[:, j - 12, :]
                        A(dst, work[:, j % 4, 0:T], ACT.Copy).then_inc(small_ok, 1)

                    def exps(h):
                        act.wait_ge(att_m, h + 1)
                        for q in range(HALVES):
                            cols = slice(q * P, q * P + (q + 1) * P)
                            n = 4 * (h % 2) + q
                            mm = A(probs[:, h % 2, cols], probs[:, h % 2, cols], ACT.Exp,
                                   bias=att_st[:, n:n + 1], scale=SCALE,
                                   accum_out=att_st[:, 8 + n:9 + n])
                        mm.then_inc(att_e, 1)

                    def emptyo(h):
                        act.wait_ge(att_o, h + 1)
                        A(xT_high[:, h, :], y[:, h % 2, 0:T],
                          ACT.Copy).then_inc(att_h, 1)
                    exps(0)
                    for h in range(HEADS):
                        if h + 1 < HEADS:
                            exps(h + 1)
                        emptyo(h)
                    in_threes(act, FIRST["mla_out"], end_of["mla_out"],
                              lambda i, c: make_high(i, c + RING))

                std(2 * layer)
                split_xT(2 * layer)
                project(f"wq{layer}", lambda i, t, bank: A(
                    queryT[:, bass.ds(i * RING + t, 1), :].rearrange("p o t -> p (o t)"),
                    work[:, bank, 0:T], ACT.Copy).then_inc(emptied, 1))
                for n in range(HALVES * HP // 4):
                    act.wait_ge(score_mm, 8 * layer + n + 1)
                    A(scores[:, 4 * n:4 * n + 4, :].rearrange("p j n -> p (j n)"), y[:, n % 4, :],
                      ACT.Copy).then_inc(score_ok, 1)

                def gelu(i, t, bank):
                    A(big[:, bass.ds(i * RING + t, 1), :].rearrange("p o t -> p (o t)"),
                      work[:, bank, 0:T], ACT.Gelu).then_inc(emptied, 1)
                u0 = FIRST[f"u{layer}"]
                for part in range(2):
                    a, b = ((u0, u0 + POOL_U), (u0 + POOL_U, u0 + NKEYS))[part]

                    def one(i, c):
                        act.wait_ge(block_used, g_of(i, c + 1))
                        gelu(i, c - u0, c % RING)
                        make_high(i, c + RING)
                    in_threes(act, a, b, one)
                    if part == 0:
                        act.wait_ge(expo_in, layer + 1)
                        A(cand_v, cand_v, ACT.Exp).then_inc(expo_ok, 1)
                v0 = FIRST[f"v{layer}"]
                act.wait_ge(gated, (layer + 1) * GROUPS)
                ln_rows(2 * layer + 1)

                def a_hi(i, c):
                    A(xT_high[:, c % RING, :],
                      big[:, bass.ds(i * RING + (c - v0), 1), :].rearrange("p o t -> p (o t)"),
                      ACT.Copy).then_inc(a_high, 1)
                for g in range(v0, v0 + RING):
                    a_hi(0, g)

                def one_v(i, c):
                    act.wait_ge(block_used, g_of(i, c + 1))
                    a_hi(i, c + RING)
                    make_high(i, c + RING)
                in_threes(act, v0, v0 + NKEYS - RING, one_v)
                if layer + 1 < DEPTH:
                    for g in range(v0 + NKEYS - RING, v0 + NKEYS):
                        make_high(0, g + RING)
                std(2 * layer + 1)

        @block.vector
        def _(dve):
            V = nc.vector
            count = [0]

            def step(ins):
                count[0] += 1
                ins.then_inc(v_step, 1)
                dve.wait_ge(v_step, count[0])

            def low_stage(a, b):
                in_threes(dve, a, b, lambda i, c: make_low(dve, V, "vector", i, c))

            def layer_norm(n):
                dve.wait_ge(ln_in[n], 16 * LN_ROWS[n])
                for h in range(HALVES):
                    xs = x[:, h, :]
                    step(V.scalar_tensor_tensor(xs, xs, ALPHA,
                                                y[:, 2 * h:2 * h + 2, :].rearrange("p b n -> p (b n)"),
                                                ALU.mult, ALU.add))
                    if LN_ROWS[n] == 3:
                        step(V.tensor_tensor(xs, xs, aux[:, 2 * D:3 * D], ALU.add))
                    V.bn_stats(stats[:, 12 * h:12 * h + 6], x[:, h, 0:512])
                    step(V.bn_stats(stats[:, 12 * h + 6:12 * h + 12], x[:, h, 512:1024]))
                    step(V.bn_aggr(stats[:, 24 + 2 * h:26 + 2 * h], stats[:, 12 * h:12 * h + 12]))
                V.tensor_scalar(stats[:, 28:30], stats[:, 25:28:2], LN_EPS, None,
                                ALU.add).then_inc(var_ok, 1)
                dve.wait_ge(std_ok, n + 1)
                step(V.reciprocal(stats[:, 32:34], stats[:, 30:32]))
                for h in range(HALVES):
                    xs = x[:, h, :]
                    step(V.tensor_scalar(xs, xs, stats[:, 24 + 2 * h:25 + 2 * h], stats[:, 32 + h:33 + h],
                                         ALU.subtract, ALU.mult))
                    step(V.tensor_tensor(xs, xs, aux[:, 0:D], ALU.mult))
                    V.tensor_tensor(xs, xs, aux[:, D:2 * D], ALU.add).then_inc(x_ready, 1)

            def split_xT(n, made):
                for h in range(HALVES):
                    dve.wait_ge(xT_hi_ok, made + h + 1)
                    V.tensor_tensor(xT_low[:, :, h * P:(h + 1) * P],
                                    work[:, 2 * h:2 * h + 2, :].rearrange("p b (k t) -> p (b k) t", t=P),
                                    xT_high[:, :, h * P:(h + 1) * P].bitcast(F32),
                                    ALU.subtract).then_inc(xT_lo_ok, 1)

            def select(layer):
                dve.wait_ge(score_ok, 8 * (layer + 1))
                base = layer * (7 * HALVES * HP + 7 * HALVES * PH)

                def top16(i, k0, per):
                    def did(ins, k):
                        ins.then_inc(v_loop, 1)
                        wait_apart(dve, v_loop, i * per + (k0 + k))
                    return did

                with dve.Fori(0, HALVES * HP) as i:
                    did = top16(i, base, 7)
                    ra, rb = row_a[:, 0:NKEYS], row_b[:, 0:NKEYS]
                    did(V.tensor_copy(ra, scores[:, bass.ds(i, 1), :].rearrange("p o n -> p (o n)")), 1)
                    did(V.max(sel_v[:, 0:8], ra), 2)
                    V.max_index(sel_i[:, 0:8], sel_v[:, 0:8], ra)
                    did(V.match_replace(rb, sel_v[:, 0:8], ra, LOWEST), 3)
                    did(V.max(sel_v[:, 8:16], rb), 4)
                    did(V.max_index(sel_i[:, 8:16], sel_v[:, 8:16], rb), 5)
                    did(V.tensor_copy(top_v[:, bass.ds(i * TOPK, TOPK)], sel_v), 6)
                    did(V.tensor_copy(top_i[:, bass.ds(i * TOPK, TOPK)], sel_i), 7)
                base += 7 * HALVES * HP
                with dve.Fori(0, HALVES * PH) as i:
                    did = top16(i, base, 7)
                    did(V.tensor_tensor(row_a.rearrange("p (a b) -> p a b", b=TOPK),
                                        top_v[:, bass.ds(i * 2 * TOPK, TOPK)].unsqueeze(2)
                                        .to_broadcast([P, TOPK, TOPK]),
                                        top_v[:, bass.ds(i * 2 * TOPK + TOPK, TOPK)].unsqueeze(1)
                                        .to_broadcast([P, TOPK, TOPK]), ALU.add), 1)
                    did(V.max(sel_v[:, 0:8], row_a), 2)
                    V.max_index(sel_i[:, 0:8], sel_v[:, 0:8], row_a)
                    did(V.match_replace(row_b, sel_v[:, 0:8], row_a, LOWEST), 3)
                    did(V.max(sel_v[:, 8:16], row_b), 4)
                    did(V.max_index(sel_i[:, 8:16], sel_v[:, 8:16], row_b), 5)
                    did(V.tensor_copy(cand_v[:, bass.ds(i * TOPK, TOPK)], sel_v), 6)
                    did(V.tensor_copy(cand_i[:, bass.ds(i * TOPK, TOPK)], sel_i), 7)
                cv = cand_v.rearrange("p (j k) -> p j k", k=TOPK)
                shape = [P, HALVES * PH, TOPK]
                step(V.tensor_copy(gate_inv, cv[:, :, 0]))
                V.tensor_tensor(cv, cv, gate_inv.unsqueeze(2).to_broadcast(shape),
                                ALU.subtract).then_inc(expo_in, 1)
                V.tensor_scalar(rank1_u, cand_i, 4, None, ALU.logical_shift_right)
                step(V.tensor_scalar(rank2_u, cand_i, TOPK - 1, None, ALU.bitwise_and))
                V.tensor_copy(rank1, rank1_u)
                step(V.tensor_copy(rank2, rank2_u))
                m4 = match.rearrange("p (h k i) -> p h k i", k=TOPK, i=TOPK)
                p4 = picked.rearrange("p (h k i) -> p h k i", k=TOPK, i=TOPK)
                full = [P, PH, TOPK, TOPK]
                for h in range(HALVES):
                    for side, rank in ((0, rank1), (1, rank2)):
                        rk = rank[:, h * P:(h + 1) * P].rearrange("p (h k) -> p h k", k=TOPK)
                        ids = top_i[:, h * HP * TOPK:(h + 1) * HP * TOPK].rearrange(
                            "p (h s i) -> p h s i", s=2, i=TOPK)[:, :, side, :]
                        step(V.tensor_tensor(match.rearrange("p (k i) -> p k i", i=TOPK),
                                             rank[:, h * P:(h + 1) * P].unsqueeze(2)
                                             .to_broadcast([P, P, TOPK]),
                                             iota[:, 0:TOPK].unsqueeze(1).to_broadcast([P, P, TOPK]),
                                             ALU.is_equal))
                        step(V.tensor_tensor(p4, m4, ids.unsqueeze(2).to_broadcast(full), ALU.mult))
                        step(V.tensor_reduce(chosen[:, side, h * P:(h + 1) * P],
                                             picked.rearrange("p (k i) -> p k i", i=TOPK),
                                             AX.X, ALU.add))
                dve.wait_ge(expo_ok, layer + 1)
                step(V.tensor_reduce(gate_sum, cv, AX.X, ALU.add))
                step(V.reciprocal(gate_inv, gate_sum))
                V.tensor_tensor(chosen[:, 2, :].rearrange("p (j k) -> p j k", k=TOPK), cv,
                                gate_inv.unsqueeze(2).to_broadcast(shape),
                                ALU.mult).then_inc(chosen_ok, 1)

            def spread(layer):
                dve.wait_ge(chosen_mm, layer + 1)
                V.tensor_copy(chosenT[:].rearrange("p q t -> p (q t)")[:, 0:512],
                              y[:, 0, :])
                V.tensor_copy(chosenT[:].rearrange("p q t -> p (q t)")[:, 512:768],
                              y[:, 1, 0:256]).then_inc(chosenT_ok, 1)
                dve.wait_ge(chosenT_ok, layer + 1)
                dve.wait_ge(emptied, PROJECTED[f"u{layer}"] + NKEYS)
                n = layer * GROUPS

                def hot2(i, q, peeled=False):
                    if not peeled:
                        dve.wait_ge(spread_ok, i + (n + q - 1))
                    s = (q % 2) * GROUP
                    for t in range(GROUP):
                        at = i * GROUP + (q * GROUP + t)
                        last = V.tensor_scalar(onehot2[:, s + t, :], iota[:],
                                               chosenT[:, 1, bass.ds(at, 1)],
                                               chosenT[:, 2, bass.ds(at, 1)],
                                               ALU.is_equal, ALU.mult)
                    last.then_inc(hot2_ok, 1)

                def gate(i, q):
                    dve.wait_ge(spread_ok, i + (n + q + 1))
                    hid = big[:, :, bass.ds(i * GROUP + q * GROUP, GROUP)].rearrange("p b t -> p t b")
                    V.tensor_tensor(hid, work[:, q % 4, :].rearrange("p (t b) -> p t b", b=NKEYS), hid,
                                    ALU.mult).then_inc(gated, 1)

                hot2(0, 0, True)
                hot2(0, 1, True)
                gate(0, 0)
                hot2(0, 2)
                gate(0, 1)
                hot2(0, 3)
                gate(0, 2)
                with dve.Fori(0, GROUPS // 4 - 1) as i:
                    for q in range(4):
                        hot2(i * 4, q + 4)
                        gate(i * 4, q + 3)
                gate(0, GROUPS - 1)

            def low_v(layer):
                v0 = FIRST[f"v{layer}"]

                def a_lo(i, c):
                    dve.wait_ge(a_high, g_of(i, c - v0 + NKEYS * layer + 1))
                    V.tensor_tensor(xT_low[:, c % RING, :],
                                    big[:, bass.ds(i * RING + (c - v0), 1), :].rearrange("p o t -> p (o t)"),
                                    xT_high[:, c % RING, :].bitcast(F32),
                                    ALU.subtract).then_inc(a_low, 1)
                for g in range(v0, v0 + RING):
                    a_lo(0, g)

                def one(i, c):
                    a_lo(i, c)
                    make_low(dve, V, "vector", i, c)
                in_threes(dve, v0 + RING, end_of[f"v{layer}"], one)
                if layer + 1 < DEPTH:
                    low_stage(end_of[f"v{layer}"], end_of[f"v{layer}"] + RING)

            dve.wait_ge(xT_hi_ok, 1)
            V.tensor_tensor(xT_low[:], xT_in.rearrange("p (k t) -> p k t", k=KD),
                            xT_high[:].bitcast(F32), ALU.subtract).then_inc(xT_lo_ok, 1)
            dve.wait_ge(consts, 4)
            dve.wait_ge(inputs_in, 32)
            for k in range(KD):
                dve.wait_ge(emptied, 2 * k + 2)
                V.tensor_tensor(padded[:, k, PAD:PAD + T], value_buf[:, k % 2, :], gate_buf[:, k % 2, :],
                                ALU.mult).then_inc(glu_ok, 1)
                dve.wait_ge(glu_ok, k + 1)
                tap = lambda w: conv_p[:, C_TAPS + k * TAPS + w:C_TAPS + k * TAPS + w + 1]
                step(V.tensor_scalar(conv[:, k, :], padded[:, k, 0:T], tap(0),
                                     conv_p[:, C_BDW + k:C_BDW + k + 1], ALU.mult, ALU.add))
                for w in range(1, TAPS):
                    ins = V.scalar_tensor_tensor(conv[:, k, :], padded[:, k, w:w + T], tap(w),
                                                 conv[:, k, :], ALU.mult, ALU.add)
                    if k == KD - 1 and w == TAPS - 1:
                        ins.then_inc(conv_done, 1)
                    else:
                        step(ins)
            over = [P, KD, T]
            dve.wait_ge(stat_mm, 1)
            step(V.tensor_scalar(mean_c, work[:, 3, 0:T], 1.0 / D, None, ALU.mult))
            V.tensor_tensor(conv[:], conv[:], mean_c.unsqueeze(1).to_broadcast(over),
                            ALU.subtract).then_inc(mean_ok, 1)
            dve.wait_ge(stat_mm, 2)
            V.tensor_scalar(var_c, work[:, 3, T:2 * T], 1.0 / D, LN_EPS, ALU.mult,
                            ALU.add).then_inc(cvar_ok, 1)
            dve.wait_ge(cstd_ok, 1)
            step(V.reciprocal(rstd_c, std_c))
            V.tensor_tensor(conv[:], conv[:], rstd_c.unsqueeze(1).to_broadcast(over),
                            ALU.mult).then_inc(norm_ok, 1)
            dve.wait_ge(xT_hi_ok, 2)
            V.tensor_tensor(xT_low[:], squares[:], xT_high[:].bitcast(F32),
                            ALU.subtract).then_inc(xT_lo_ok, 1)
            low_stage(FIRST["conv_out"] + RING, end_of["conv_out"] + RING)
            dve.wait_ge(x_in, 16 * HALVES)
            dve.wait_ge(block_used, end_of["conv_out"])

            for layer in range(DEPTH):
                if layer == 1:
                    split_xT(1, 4)
                    dve.wait_ge(mla_in, 16 * 5)
                    step(V.tensor_copy(angle, pos_i))
                    step(V.tensor_scalar(angle, angle, mla_p[:, M_FREQ:M_FREQ + 1], None, ALU.mult))
                    big_half = 1.5 * 2.0 ** 23
                    step(V.tensor_scalar(turns, angle, 0.15915494309189535, big_half, ALU.mult, ALU.add))
                    step(V.tensor_scalar(turns, turns, big_half, None, ALU.subtract))
                    step(V.tensor_scalar(turns_hi, turns, 1.0 / 4096, big_half, ALU.mult, ALU.add))
                    step(V.tensor_scalar(turns_hi, turns_hi, big_half, 4096.0, ALU.subtract, ALU.mult))
                    step(V.tensor_tensor(turns_lo, turns, turns_hi, ALU.subtract))
                    for part in TWO_PI_PARTS:
                        for k in (turns_hi, turns_lo):
                            step(V.scalar_tensor_tensor(angle, k, -part, angle, ALU.mult, ALU.add))
                    step(V.tensor_scalar(angle, angle, 3.1415925, -3.1415925, ALU.min, ALU.max))
                    step(V.tensor_scalar(spare, angle, -1.0, None, ALU.mult))
                    step(V.tensor_tensor(spare, spare, angle, ALU.max))
                    V.tensor_scalar(turns, spare, -1.0, 1.5707963267948966, ALU.mult,
                                    ALU.add).then_inc(ang_ok, 1)
                    dve.wait_ge(rms_mm, 1)
                    V.tensor_scalar(rms[:, 0, :], work[:, 3, 0:T], 1.0 / Q_RANK, RMS_EPS,
                                    ALU.mult, ALU.add)
                    V.tensor_scalar(rms[:, 1, :], work[:, 3, T:2 * T], 1.0 / KV_RANK, RMS_EPS,
                                    ALU.mult, ALU.add).then_inc(rms_var, 1)
                    dve.wait_ge(rms_std, 1)
                    step(V.reciprocal(rms[:], rms[:]))
                    for k in range(KQ + KKV):
                        last = V.scalar_tensor_tensor(latent_n[:, k, :], latent[:, k, :],
                                                      mla_p[:, k:k + 1], rms[:, int(k >= KQ), :],
                                                      ALU.mult, ALU.mult)
                    last.then_inc(lat_ok, 1)

                    def turn(dst, src, n):
                        for s in range(n):
                            a, b = src[:, 2 * s, :], src[:, 2 * s + 1, :]
                            V.tensor_tensor(turn_tmp[:, 0, :], b, sinT, ALU.mult)
                            V.tensor_tensor(turn_tmp[:, 1, :], a, sinT, ALU.mult)
                            V.tensor_tensor(dst[:, 2 * s, :], a, cosT, ALU.mult)
                            step(V.tensor_tensor(dst[:, 2 * s + 1, :], b, cosT, ALU.mult))
                            V.tensor_tensor(dst[:, 2 * s, :], dst[:, 2 * s, :], turn_tmp[:, 0, :],
                                            ALU.subtract)
                            step(V.tensor_tensor(dst[:, 2 * s + 1, :], dst[:, 2 * s + 1, :],
                                                 turn_tmp[:, 1, :], ALU.add))
                    dve.wait_ge(trig_ok, 1)
                    turn(k_turned, k_rot, 1)
                    dve.wait_ge(consts, 4 + 3)
                    for q in range(4):
                        rows = slice(32 * q, 32 * (q + 1))
                        last = V.tensor_copy(k_masked[rows, q, :, :], k_turned[rows, :, :])
                    step(last)
                    dve.wait_ge(small_ok, 4)
                    turn(q_turned, queries, 2)
                    for h in range(HALVES):
                        dve.wait_ge(value_mm, h + 1)
                        V.tensor_copy(values[:, h, :], y[:, 2 * h:2 * h + 2, :].rearrange("p b n -> p (b n)")
                                      ).then_inc(value_ok, 1)
                    V.memset(att_st[:, 16:17], 0.0).then_inc(q_turn_ok, 1)

                    def maxima(h):
                        dve.wait_ge(att_s, h + 1)
                        if h >= 2:
                            dve.wait_ge(att_t, h - 1)
                        step(V.tensor_tensor(probs[:, h % 2, :], work[:, h % 2, 0:3 * P], mask, ALU.add))
                        n = 4 * (h % 2)
                        V.tensor_reduce(att_st[:, 20:21], probs[:, h % 2, 0:P], AX.X, ALU.max)
                        step(V.tensor_reduce(att_st[:, 21:22], probs[:, h % 2, P:3 * P], AX.X, ALU.max))
                        V.tensor_scalar(att_st[:, n:n + 2], att_st[:, 20:22], -SCALE, None,
                                        ALU.mult).then_inc(att_m, 1)

                    def normalise(h):
                        dve.wait_ge(att_e, h + 1)
                        n = 4 * (h % 2)
                        step(V.reciprocal(att_st[:, 24:26], att_st[:, 8 + n:10 + n]))
                        V.tensor_scalar(probs[:, h % 2, 0:P], probs[:, h % 2, 0:P], att_st[:, 24:25],
                                        None, ALU.mult)
                        V.tensor_scalar(probs[:, h % 2, P:3 * P], probs[:, h % 2, P:3 * P],
                                        att_st[:, 25:26], None, ALU.mult).then_inc(att_p, 1)

                    def copies(h):
                        dve.wait_ge(att_t, h + 1)
                        if h >= 2:
                            dve.wait_ge(att_o, h - 1)
                        V.tensor_copy(probsT[:, h % 2, :], work[:, 2, 0:3 * P]).then_inc(att_c, 1)

                    def out_low(h):
                        dve.wait_ge(att_h, h + 1)
                        V.tensor_tensor(xT_low[:, h, :], y[:, h % 2, 0:T],
                                        xT_high[:, h, :].bitcast(F32), ALU.subtract).then_inc(att_l, 1)
                    maxima(0)
                    for h in range(HEADS):
                        if h + 1 < HEADS:
                            maxima(h + 1)
                        normalise(h)
                        copies(h)
                        if h >= 1:
                            out_low(h - 1)
                    out_low(HEADS - 1)
                    low_stage(FIRST["mla_out"] + RING, end_of["mla_out"] + RING)
                    dve.wait_ge(block_used, end_of["mla_out"])

                layer_norm(2 * layer)
                split_xT(2 * layer, (2, 6)[layer])
                low_stage(FIRST[f"wq{layer}"] + RING, end_of[f"wq{layer}"] + RING)
                select(layer)
                low_stage(FIRST[f"u{layer}"] + RING + POOL_U, end_of[f"u{layer}"] + RING)
                spread(layer)
                low_v(layer)
                dve.wait_ge(block_used, end_of[f"v{layer}"])
                layer_norm(2 * layer + 1)


def _two_pi_parts():
    import math
    parts, rest = [6.28125], 2 * math.pi - 6.28125
    for _ in range(2):
        scale = 2.0 ** (10 - math.floor(math.log2(rest)))
        parts.append(math.floor(rest * scale) / scale)
        rest -= parts[-1]
    return parts + [rest]


TWO_PI_PARTS = _two_pi_parts()


def kernel(x, positions, conv_w_in, conv_b_in, conv_w_dw, conv_b_dw, conv_ln_g, conv_ln_b,
           conv_w_out, conv_b_out, mla_w_in, mla_q_norm, mla_kv_norm, mla_w_uq, mla_w_uk,
           mla_w_uv, mla_w_out, peer_w_q, peer_sub_keys, peer_u, peer_v,
           ln1_g, ln1_b, ln2_g, ln2_b):
    import numpy as np
    import concourse.bacc as bacc
    from concourse.bass_utils import run_bass_kernel_spmd

    arr = {k: np.asarray(v) for k, v in dict(
        x=x, positions=positions, conv_w_in=conv_w_in, conv_b_in=conv_b_in, conv_w_dw=conv_w_dw,
        conv_b_dw=conv_b_dw, conv_ln_g=conv_ln_g, conv_ln_b=conv_ln_b, conv_w_out=conv_w_out,
        conv_b_out=conv_b_out, mla_w_in=mla_w_in, mla_q_norm=mla_q_norm, mla_kv_norm=mla_kv_norm,
        mla_w_uq=mla_w_uq, mla_w_uk=mla_w_uk, mla_w_uv=mla_w_uv, mla_w_out=mla_w_out,
        peer_w_q=peer_w_q, peer_sub_keys=peer_sub_keys, peer_u=peer_u, peer_v=peer_v,
        ln1_g=ln1_g, ln1_b=ln1_b, ln2_g=ln2_g, ln2_b=ln2_b).items()}

    def stationary(w):
        n = w.shape[1] // P
        return w.reshape(KD, P, n, P).transpose(2, 1, 0, 3).reshape(n, P, KD * P)

    def per_channel(v):
        return v.reshape(-1, P).T

    xr = arr["x"][0]
    w_in = arr["conv_w_in"][0]
    conv_in = stationary(w_in).reshape(2, KD, P, D).transpose(1, 0, 2, 3).reshape(2 * KD, P, D)
    conv_par = np.concatenate(
        [per_channel(arr["conv_b_in"][0]), per_channel(arr["conv_b_dw"][0]),
         per_channel(arr["conv_ln_g"][0]), per_channel(arr["conv_ln_b"][0]),
         arr["conv_w_dw"][0].reshape(TAPS, KD, P).transpose(2, 1, 0).reshape(P, KD * TAPS)], axis=1)

    w = arr["mla_w_in"][0]
    half = ROPE // 2
    r0 = Q_RANK + KV_RANK
    mla_in = stationary(np.concatenate(
        [w[:, :r0], np.tile(w[:, r0:r0 + half], 4), np.tile(w[:, r0 + half:r0 + ROPE], 4)], axis=1))
    uq = arr["mla_w_uq"][0].reshape(Q_RANK, HEADS, NOPE + ROPE)
    rot = [uq[:, 4 * g:4 * g + 4, NOPE + half * s:NOPE + half * (s + 1)].reshape(Q_RANK, P)
           for g in range(2) for s in range(2)]
    uq = np.stack(rot + [uq[:, h, :NOPE] for h in range(HEADS)])
    w_uq = uq.reshape(12, KQ, P, P).transpose(2, 0, 1, 3)
    w_uk = arr["mla_w_uk"][0].reshape(KKV, P, HEADS, P).transpose(1, 2, 0, 3)
    w_uv = arr["mla_w_uv"][0].reshape(KKV, P, D).transpose(1, 0, 2)
    freq = (1.0 / (np.float32(10000.0) ** (np.arange(0, ROPE, 2, dtype=np.float32)
                                           / np.float32(ROPE)))).astype(np.float32)
    mla_par = np.concatenate([per_channel(arr["mla_q_norm"][0]), per_channel(arr["mla_kv_norm"][0]),
                              np.tile(freq, 4)[:, None]], axis=1)

    ln_par = np.stack([np.stack([arr["ln1_g"][0], arr["ln1_b"][0], arr["conv_b_out"][0]]),
                       np.stack([arr["ln2_g"][0], arr["ln2_b"][0], arr["ln2_b"][0]]),
                       np.stack([arr["ln1_g"][1], arr["ln1_b"][1], arr["ln1_b"][1]]),
                       np.stack([arr["ln2_g"][1], arr["ln2_b"][1], arr["ln2_b"][1]])])
    experts = NKEYS * NKEYS
    ins = {
        "x_rows": xr.reshape(HALVES, P, D),
        "x_cols": xr.reshape(T, KD, P).transpose(2, 1, 0),
        "positions": arr["positions"].reshape(1, T),
        "conv_par": conv_par,
        "mla_par": mla_par,
        "ln_par": ln_par,
        "keys": arr["peer_sub_keys"].transpose(0, 3, 1, 2),
        "w_uq": w_uq, "w_uk": w_uk, "w_uv": w_uv,
        "conv_in": conv_in,
        "conv_out": arr["conv_w_out"][0].reshape(KD, P, D),
        "mla_in": mla_in,
        "mla_out": arr["mla_w_out"][0].reshape(KD, P, D),
        "wq": np.stack([stationary(arr["peer_w_q"][n]) for n in range(DEPTH)]),
        "u": arr["peer_u"].reshape(DEPTH, experts // P, P, KD, P).transpose(0, 1, 4, 3, 2)
        .reshape(DEPTH, experts // P, P, KD * P),
        "v": arr["peer_v"].reshape(DEPTH, experts // P, P, D),
    }
    ins = {k: np.ascontiguousarray(v) for k, v in ins.items()}

    nc = bacc.Bacc("TRN2", target_bir_lowering=False, num_devices=1)
    aps = {k: nc.dram_tensor(k, v.shape, mybir.dt.from_np(v.dtype), kind="ExternalInput").ap()
           for k, v in ins.items()}
    out = nc.dram_tensor("out", (HALVES, P, D), F32, kind="ExternalOutput").ap()
    names = ("conv_in", "conv_out", "mla_in", "mla_out", "wq", "u", "v")
    rest = [aps[k] for k in ins if k not in names]
    program(nc, *rest, {k: aps[k] for k in names}, out)
    r = run_bass_kernel_spmd(nc, [ins], core_ids=[0])
    return r.results[0]["out"].reshape(1, T, D)
```

```python
from contextlib import ExitStack

import concourse.bass as bass
from concourse import mybir

F32 = mybir.dt.float32
F32R = mybir.dt.float32r
F16 = mybir.dt.float16
I32 = mybir.dt.int32
U32 = mybir.dt.uint32
ACT = mybir.ActivationFunctionType
ALU = mybir.AluOpType
AX = mybir.AxisListType

P = 128
D = 1024
T = 256
HALVES = T // P
KD = D // P
DEPTH = 2
ALPHA = float((2 * DEPTH) ** 0.25)
LN_EPS = 1e-5
RMS_EPS = 1e-6

TAPS = 31
PAD = TAPS - 1
ROW = PAD + T + 2

HEADS = 8
NOPE, ROPE = 128, 64
Q_RANK, KV_RANK = 384, 256
KQ, KKV = Q_RANK // P, KV_RANK // P
CHUNK = 64
SCALE = float((NOPE + ROPE) ** -0.5)
MASKED = -1e30

PH = 8
NKEYS = 128
TOPK = 16
HP = 2 * PH
LOWEST = -3.0e38

RING = 3
SPLIT = 80
BATCH = 8
BATCHES = T // BATCH
ROUNDS = BATCHES // 2
WIDTHS = [(0, SPLIT), (SPLIT, NKEYS)]
GATE_SCALE = 2.0 ** 15
assert RING * ROUNDS == NKEYS - SPLIT

STREAM = [("conv_in", 2 * KD), ("conv_out", KD), ("wq0", HP), ("u0", NKEYS), ("v0", NKEYS),
          ("mla_in", KQ + KKV + 2), ("mla_out", KD), ("wq1", HP), ("u1", NKEYS), ("v1", NKEYS)]
FIRST, BLOCKS = {}, {}
_g = 0
for _name, _n in STREAM:
    FIRST[_name], BLOCKS[_name] = _g, _n
    _g += _n
TOTAL = _g

LOW_BY = []
_cuts = [(0, "pool"), (FIRST["conv_out"] + RING, "vector")]
for _l in range(DEPTH):
    _cuts += [(FIRST[f"u{_l}"] + RING, "pool"), (FIRST[f"v{_l}"] + RING * (ROUNDS + 1), "vector")]
    if _l == 0:
        _cuts += [(FIRST["mla_in"] + RING, "pool"), (FIRST["mla_out"] + RING, "vector")]
_made = {"pool": 0, "vector": 0}
for _i, (_a, _who) in enumerate(_cuts):
    _b = _cuts[_i + 1][0] if _i + 1 < len(_cuts) else TOTAL
    LOW_BY.append((_a, _b, _who, _made[_who]))
    _made[_who] += _b - _a

PROJECTED = {"conv_in": 0, "wq0": 2 * KD, "u0": 2 * KD + HP, "mla_in": 2 * KD + HP + NKEYS}
PROJECTED["wq1"] = PROJECTED["mla_in"] + BLOCKS["mla_in"]
PROJECTED["u1"] = PROJECTED["wq1"] + HP

C_BIN, C_BDW, C_LNG, C_LNB, C_TAPS = 0, 2 * KD, 3 * KD, 4 * KD, 5 * KD
CONV_COLS = 5 * KD + KD * TAPS
M_QN, M_KVN, M_FREQ = 0, KQ, KQ + KKV
MLA_COLS = KQ + KKV + 1
LN_ROWS = [3, 2, 2, 2]


def low_parts(a, b):
    for lo, hi, who, made in LOW_BY:
        if max(a, lo) < min(b, hi):
            yield max(a, lo), min(b, hi), who, made - lo


def in_threes(eng, a, b, body):
    rounds = (b - a) // RING
    if rounds >= 2:
        with eng.Fori(0, rounds) as i:
            for r in range(RING):
                body(i, a + r)
        a += RING * rounds
    for g in range(a, b):
        body(0, g)


def in_rounds(eng, a, rounds, body):
    for r in range(RING):
        body(0, 0, a + r, r)
    with eng.Fori(0, rounds - 2) as i:
        for r in range(RING):
            body(i, 1, a + RING + r, r)
    for r in range(RING):
        body(0, rounds - 1, a + RING * (rounds - 1) + r, r)


def program(nc, x_rows, x_cols, positions, conv_par, mla_par, ln_par, keys, w_uq, w_uk, w_uv,
            blocks, out):
    with ExitStack() as ctx:
        def sb(name, shape, dtype=F32):
            return ctx.enter_context(nc.sbuf_tensor(name, shape, dtype))

        def sem(name):
            return ctx.enter_context(nc.semaphore(name))

        big = sb("big", [P, NKEYS, T])
        raw = sb("raw", [P, RING, D])
        high = sb("high", [P, RING, D], F32R)
        low = sb("low", [P, RING, D], F32R)
        xT_high = sb("xT_high", [P, KD, T], F32R)
        xT_low = sb("xT_low", [P, KD, T], F32R)
        x = sb("x", [P, HALVES, D])
        aux = sb("aux", [P, 3 * D])
        iota = sb("iota", [P, P])
        ident = sb("ident", [P, P])
        ones = sb("ones", [P, P])
        chosenT = sb("chosenT", [P, 4, T], F16)
        iota_b = sb("iota_b", [P, P * BATCH], F16)
        onehot2 = sb("onehot2", [P, P * BATCH], F16)
        stats = sb("stats", [P, 64])

        work = ctx.enter_context(nc.psum_tensor("work", [P, 4, 512], F32))
        y = ctx.enter_context(nc.psum_tensor("y", [P, 4, 512], F32))

        def room(slot, width, dtype=None):
            flat = big[:].rearrange("p b t -> p (b t)")[:, slot * T:slot * T + width]
            return flat if dtype is None else flat.bitcast(dtype)

        xT_in = room(0, KD * T)
        conv_p = room(8, CONV_COLS)
        value_buf = room(10, 2 * T).rearrange("p (s t) -> p s t", s=2)
        gate_buf = room(12, 2 * T).rearrange("p (s t) -> p s t", s=2)
        padded = room(14, KD * ROW).rearrange("p (k t) -> p k t", k=KD)
        conv = room(24, KD * T).rearrange("p (k t) -> p k t", k=KD)
        squares = room(32, KD * T).rearrange("p (k t) -> p k t", k=KD)
        mean_c, var_c, std_c, rstd_c = (room(40 + n, T) for n in range(4))

        keysT = room(73, 2 * NKEYS).rearrange("p (s n) -> p s n", s=2)
        queryT = room(112, HP * T).rearrange("p (j t) -> p j t", j=HP)
        scores = room(96, HALVES * HP * NKEYS).rearrange("p (j n) -> p j n", n=NKEYS)
        top_v = room(80, HALVES * HP * TOPK)
        top_i = room(82, HALVES * HP * TOPK)
        cand_v = room(84, HALVES * PH * TOPK)
        cand_i = room(85, HALVES * PH * TOPK, U32)
        rank1_u, rank2_u = room(86, T, U32), room(87, T, U32)
        rank1, rank2 = room(88, T), room(89, T)
        sel_v = room(90, TOPK)
        sel_i = room(91, TOPK, U32)
        row_a, row_b = room(92, T), room(93, T)
        gate_sum = room(94, HALVES * PH)
        gate_inv = room(95, HALVES * PH)
        match = room(96, PH * TOPK * TOPK)
        picked = room(104, PH * TOPK * TOPK)
        onehots = aux[:].bitcast(F16).rearrange("p (s q n) -> p s q n", s=2, q=3)
        chosen = aux[:, 16 * P:16 * P + 3 * T].rearrange("p (q t) -> p q t", q=3)

        latent = room(0, (KQ + KKV) * T).rearrange("p (k t) -> p k t", t=T)
        k_rot = room(5, 2 * T).rearrange("p (s t) -> p s t", s=2)
        lat_sq = room(7, (KQ + KKV) * T).rearrange("p (k t) -> p k t", t=T)
        pos_i = room(12, T, I32)
        angle, turns, turns_hi, turns_lo = (room(13 + n, T) for n in range(4))
        spare = room(17, T)
        cosT, sinT = room(18, T), room(19, T)
        rms = room(20, 2 * T).rearrange("p (s t) -> p s t", s=2)
        latent_n = room(22, (KQ + KKV) * T).rearrange("p (k t) -> p k t", t=T)
        k_turned = room(27, 2 * T).rearrange("p (s t) -> p s t", s=2)
        mla_p = room(29, MLA_COLS)
        mask = room(30, 3 * P)
        queries = room(32, 12 * T).rearrange("p (j t) -> p j t", t=T)
        q_turned = room(44, 4 * T).rearrange("p (j t) -> p j t", t=T)
        turn_tmp = room(48, 2 * T).rearrange("p (s t) -> p s t", s=2)
        keys_n = room(50, HEADS * T).rearrange("p (j t) -> p j t", t=T)
        values = room(58, HALVES * D).rearrange("p (h n) -> p h n", n=D)
        probs = room(66, 2 * 3 * P).rearrange("p (s n) -> p s n", s=2)
        probsT = room(69, 2 * 3 * P).rearrange("p (s n) -> p s n", s=2)
        att_st = room(72, 64)
        uq_w = room(74, 12 * KQ * P).rearrange("p (j k c) -> p j k c", k=KQ, c=P)
        uk_w = room(92, HEADS * KKV * P).rearrange("p (j k c) -> p j k c", k=KKV, c=P)
        uv_w = room(100, KKV * D).rearrange("p (k n) -> p k n", n=D)
        k_masked = room(108, 4 * 2 * T).rearrange("p (q s t) -> p q s t", q=4, s=2)

        landed = [sem(f"block_landed_{s}") for s in range(RING)]
        high_made = sem("high_made")
        low_made = {"pool": sem("low_made_by_pool"), "vector": sem("low_made_by_vector")}
        block_used = sem("block_used")
        emptied = sem("emptied")
        inputs_in = sem("inputs_in")
        keys_in = sem("keys_in")
        x_in = sem("x_in")
        ln_in = [sem(f"ln_rows_in_{n}") for n in range(2 * DEPTH)]
        mla_in = sem("mla_weights_in")
        consts = sem("constants_made")
        pool_fill = sem("pool_fill")
        a_high = sem("a_high_made")
        a_low = sem("a_low_made")
        x_ready = sem("x_normalised")
        x_turned = sem("x_transposed")
        xT_hi_ok = sem("xT_high_made")
        xT_lo_ok = sem("xT_low_made")
        var_ok = sem("variance_made")
        std_ok = sem("std_made")
        v_step = sem("vector_step")
        v_loop = sem("vector_loop_step")
        a_step = sem("scalar_step")
        glu_ok = sem("glu_made")
        conv_done = sem("conv_done")
        stat_mm = sem("column_sums_made")
        mean_ok = sem("centred")
        sq_ok = sem("squares_made")
        cvar_ok = sem("conv_variance_made")
        cstd_ok = sem("conv_std_made")
        norm_ok = sem("conv_normalised")
        silu_ok = sem("silu_made")
        score_mm = sem("scores_made")
        score_ok = sem("scores_copied")
        expo_in = sem("gates_centred")
        expo_ok = sem("gates_exponentiated")
        chosen_ok = sem("experts_chosen")
        chosen_mm = sem("chosen_transposed")
        chosenT_ok = sem("chosen_copied")
        hot2_ok = sem("onehot2_made")
        hots_ok = sem("onehots_made")
        spread_ok = sem("gates_spread")
        gated = sem("hidden_gated")
        lat_sq_ok = sem("latent_squares")
        rms_mm = sem("rms_sums")
        rms_var = sem("rms_variance")
        rms_std = sem("rms_std")
        lat_ok = sem("latent_normalised")
        ang_ok = sem("angles_made")
        trig_ok = sem("sines_made")
        small_mm = sem("small_projection")
        small_ok = sem("small_emptied")
        value_mm = sem("values_made")
        value_ok = sem("values_copied")
        q_turn_ok = sem("queries_turned")
        att_s = sem("attention_scores")
        att_m = sem("attention_max")
        att_e = sem("attention_exp")
        att_p = sem("attention_probs")
        att_t = sem("attention_transposed")
        att_c = sem("attention_probsT")
        att_o = sem("attention_out")
        att_h = sem("attention_out_high")
        att_l = sem("attention_out_low")
        out_ok = sem("output_stored")
        waits_taken = sem("waits_taken")

        def g_of(i, c):
            return i * RING + c

        def wait_apart(eng, semaphore, value):
            eng.wait_ge(semaphore, value)
            if not isinstance(value, int):
                eng.sem_inc(waits_taken, 1)

        def batches_before(layer, phase):
            return (2 * layer + phase) * BATCHES

        def token_parts(rows):
            return rows.rearrange("p (i t) -> p t i", t=BATCH)

        def spread_banks(phase, b):
            lo, hi = WIDTHS[phase]
            if phase == 0:
                bank = y[:, 2 * (b % 2):2 * (b % 2) + 2, 0:(hi - lo) * BATCH // 2]
            else:
                bank = work[:, b % 2:b % 2 + 1, 0:(hi - lo) * BATCH]
            return bank.rearrange("p u (t b) -> p u t b", b=hi - lo)

        end_of = {name: FIRST[name] + BLOCKS[name] for name in FIRST}
        block = ctx.enter_context(nc.Block())

        @block.sync
        def _(sp):
            sp.dma_start(xT_in.rearrange("p (k t) -> p k t", k=KD), x_cols).then_inc(inputs_in, 16)
            sp.dma_start(conv_p, conv_par).then_inc(inputs_in, 16)

            def load(name, i, c):
                slot = c % RING
                src = blocks[name[:-1] if name[-1] in "01" else name]
                at = i * RING + (c - FIRST[name])
                if name[-1] in "01":
                    src = src[int(name[-1])]
                sp.dma_start(raw[:, slot, :],
                             src[bass.ds(at, 1)].rearrange("o p c -> p (o c)")).then_inc(landed[slot], 16)

            for g in range(RING):
                load("conv_in", 0, g)
            for name, _ in STREAM:
                a = max(FIRST[name], RING)
                for lo, hi, who, offset in low_parts(a - RING, end_of[name] - RING):
                    def one(i, c):
                        wait_apart(sp, high_made, g_of(i, c - RING + 1))
                        wait_apart(sp, low_made[who], g_of(i, c - RING + 1 + offset))
                        load(name, i, c)
                    in_threes(sp, lo + RING, hi + RING, one)
            for h in range(HALVES):
                sp.wait_ge(x_ready, 2 * (2 * DEPTH - 1) + h + 1)
                sp.dma_start(out[h], x[:, h, :]).then_inc(out_ok, 16)
            sp.wait_ge(out_ok, 16 * HALVES)

        def make_low(eng, ops, who, i, c):
            slot = c % RING
            eng.wait_ge(high_made, g_of(i, c + 1))
            ops.tensor_tensor(low[:, slot, :], raw[:, slot, :], high[:, slot, :].bitcast(F32),
                              ALU.subtract).then_inc(low_made[who], 1)

        @block.gpsimd
        def _(pool):
            def low_stage(name_from, a, b):
                in_threes(pool, a, b, lambda i, c: make_low(pool, nc.gpsimd, "pool", i, c))

            nc.gpsimd.iota(iota[:], [[1, P]], base=0, channel_multiplier=0,
                           allow_small_or_imprecise_dtypes=True).then_inc(consts, 1)
            nc.gpsimd.memset(ident[:], 0.0).then_inc(pool_fill, 1)
            nc.gpsimd.memset(ones[:], 1.0).then_inc(consts, 1)
            nc.gpsimd.memset(padded[:, :, 0:PAD], 0.0).then_inc(consts, 1)
            pool.wait_ge(pool_fill, 1)
            nc.gpsimd.affine_select(out=ident[:], in_=ident[:], compare_op=ALU.not_equal, fill=1.0,
                                    base=0, pattern=[[-1, P]], channel_multiplier=1).then_inc(consts, 1)
            low_stage("conv_in", 0, FIRST["conv_out"] + RING)
            for layer in range(DEPTH):
                low_stage("u", FIRST[f"u{layer}"] + RING, FIRST[f"v{layer}"] + RING * (ROUNDS + 1))
                if layer == 0:
                    pool.wait_ge(block_used, end_of["v0"])
                    nc.gpsimd.memset(mask, 0.0).then_inc(pool_fill, 1)
                    nc.gpsimd.memset(room(108, 4 * 2 * T), 0.0).then_inc(consts, 1)
                    pool.wait_ge(pool_fill, 2)
                    nc.gpsimd.memset(mask[0:CHUNK, CHUNK:P], MASKED).then_inc(consts, 1)
                    nc.gpsimd.memset(mask[0:CHUNK, 3 * P - CHUNK:3 * P], MASKED).then_inc(consts, 1)
                    low_stage("mla_in", FIRST["mla_in"] + RING, FIRST["mla_out"] + RING)

        @block.tensor
        def _(pe):
            def wait_low(who, offset, i, c):
                pe.wait_ge(low_made[who], g_of(i, c + 1 + offset))

            def project_block(name, who, offset, i, c):
                first = FIRST[name]
                wait_low(who, offset, i, c)
                if not (c < first + RING):
                    pe.wait_ge(emptied, g_of(i, c - RING + 1 - first + PROJECTED[name]))
                s = c % RING
                for k in range(KD):
                    cols = slice(k * P, (k + 1) * P)
                    for n, (w, m) in enumerate(((high, xT_high), (high, xT_low), (low, xT_high))):
                        mm = nc.tensor.matmul(work[:, s, 0:T], w[:, s, cols], m[:, k, :],
                                              start=(k == 0 and n == 0),
                                              stop=(k == KD - 1 and n == 2))
                mm.then_inc(block_used, 1)

            def project(name, blocks=None):
                first = FIRST[name]
                for lo, hi, who, offset in low_parts(first, first + (blocks or BLOCKS[name])):
                    def one(i, c):
                        project_block(name, who, offset, i, c)
                    head = min(hi, first + RING)
                    for g in range(lo, head):
                        one(0, g)
                    in_threes(pe, max(lo, head), hi, one)

            def combine_block(a_slot, s, start, stop):
                for h in range(HALVES):
                    rows = slice(h * P, (h + 1) * P)
                    for n, (a, v) in enumerate(((xT_high, high), (xT_high, low), (xT_low, high))):
                        for m in range(2):
                            mm = nc.tensor.matmul(y[:, 2 * h + m, :], a[:, a_slot, rows],
                                                  v[:, s, m * 512:(m + 1) * 512],
                                                  start=(start and n == 0), stop=(stop and n == 2))
                mm.then_inc(block_used, 1)

            def combine_all(name):
                for lo, hi, who, offset in low_parts(FIRST[name], end_of[name]):
                    for g in range(lo, hi):
                        wait_low(who, offset, 0, g)
                        t = g - FIRST[name]
                        combine_block(t, g % RING, t == 0, t == KD - 1)

            def column_sums(bank, col, src, chunks):
                for n, k in enumerate(chunks):
                    mm = nc.tensor.matmul(work[:, bank, col:col + T], ones[:], src[:, k, :],
                                          start=(n == 0), stop=(n == len(chunks) - 1))
                return mm

            def turn_x(n):
                for h in range(HALVES):
                    pe.wait_ge(x_ready, HALVES * n + h + 1)
                    for k in range(KD):
                        mm = nc.tensor.transpose(work[:, 2 * h + k // 4, (k % 4) * P:(k % 4 + 1) * P],
                                                 x[:, h, k * P:(k + 1) * P], ident[:])
                    mm.then_inc(x_turned, 1)

            def wait_xT(n):
                pe.wait_ge(xT_hi_ok, n)
                pe.wait_ge(xT_lo_ok, n)

            wait_xT(1)
            project("conv_in")
            pe.wait_ge(consts, 4)
            pe.wait_ge(conv_done, 1)
            column_sums(3, 0, conv, range(KD)).then_inc(stat_mm, 1)
            pe.wait_ge(sq_ok, 1)
            pe.wait_ge(mean_ok, 1)
            column_sums(3, T, squares, range(KD)).then_inc(stat_mm, 1)
            wait_xT(2)
            combine_all("conv_out")

            for layer in range(DEPTH):
                if layer == 1:
                    wait_xT(6)
                    project("mla_in")
                    pe.wait_ge(lat_sq_ok, 1)
                    column_sums(3, 0, lat_sq, range(KQ))
                    column_sums(3, T, lat_sq, range(KQ, KQ + KKV)).then_inc(rms_mm, 1)
                    pe.wait_ge(lat_ok, 1)
                    pe.wait_ge(mla_in, 16 * 5)
                    done = 0
                    for j in range(12 + HEADS):
                        if j >= 4:
                            pe.wait_ge(small_ok, j - 3)
                        elif j < 3:
                            pe.wait_ge(emptied, PROJECTED["wq1"])
                        w, chunks, k0 = (uq_w[:, j], KQ, 0) if j < 12 else (uk_w[:, j - 12], KKV, KQ)
                        for k in range(chunks):
                            mm = nc.tensor.matmul(work[:, j % 4, 0:T], w[:, k, :], latent_n[:, k0 + k, :],
                                                  start=(k == 0), stop=(k == chunks - 1))
                        mm.then_inc(small_mm, 1)
                    for h in range(HALVES):
                        for m in range(2):
                            for k in range(KKV):
                                mm = nc.tensor.matmul(y[:, 2 * h + m, :],
                                                      latent_n[:, KQ + k, h * P:(h + 1) * P],
                                                      uv_w[:, k, m * 512:(m + 1) * 512],
                                                      start=(k == 0), stop=(k == KKV - 1))
                        mm.then_inc(value_mm, 1)

                    def att_scores(h):
                        if h >= 2:
                            pe.wait_ge(att_m, h - 1)
                        for q in range(HALVES):
                            n = (q + 1) * P
                            cols = slice(q * P, q * P + n)
                            rows = slice(q * P, (q + 1) * P)
                            nc.tensor.matmul(work[:, h % 2, cols], queries[:, 4 + h, rows],
                                             keys_n[:, h, 0:n], start=True, stop=False)
                            for s in range(2):
                                mm = nc.tensor.matmul(work[:, h % 2, cols],
                                                      q_turned[:, 2 * (h // 4) + s, rows],
                                                      k_masked[:, h % 4, s, 0:n],
                                                      start=False, stop=(s == 1))
                        mm.then_inc(att_s, 1)

                    def att_out(h):
                        pe.wait_ge(att_p, h + 1)
                        if h >= 1:
                            pe.wait_ge(att_c, h)
                        for q in range(3):
                            mm = nc.tensor.transpose(work[:, 2, q * P:(q + 1) * P],
                                                     probs[:, h % 2, q * P:(q + 1) * P], ident[:])
                        mm.then_inc(att_t, 1)

                    def att_mix(h):
                        pe.wait_ge(att_c, h + 1)
                        if h >= 2:
                            pe.wait_ge(att_l, h - 1)
                        for q, key, start, stop in ((0, 0, True, True), (1, 0, True, False), (1, 1, False, True)):
                            mm = nc.tensor.matmul(y[:, h % 2, q * P:(q + 1) * P],
                                                  values[:, key, h * P:(h + 1) * P],
                                                  probsT[:, h % 2, (q + key) * P:(q + key + 1) * P],
                                                  start=start, stop=stop)
                        mm.then_inc(att_o, 1)

                    pe.wait_ge(small_ok, 12 + HEADS)
                    pe.wait_ge(q_turn_ok, 1)
                    pe.wait_ge(value_ok, 2)
                    att_scores(0)
                    att_scores(1)
                    for h in range(HEADS):
                        att_out(h)
                        if h + 2 < HEADS:
                            att_scores(h + 2)
                        att_mix(h)
                    pe.wait_ge(att_h, HEADS)
                    pe.wait_ge(att_l, HEADS)
                    combine_all("mla_out")

                turn_x(2 * layer)
                wait_xT((4, 8)[layer])
                project(f"wq{layer}")
                pe.wait_ge(emptied, PROJECTED[f"wq{layer}"] + HP)
                pe.wait_ge(keys_in, 16 * (layer + 1))
                for h in range(HALVES):
                    for j in range(HP):
                        if j % 4 == 0 and h == 1:
                            pe.wait_ge(score_ok, 8 * layer + j // 4 + 1)
                        mm = nc.tensor.matmul(y[:, j // 4, (j % 4) * P:(j % 4 + 1) * P],
                                              queryT[:, j, h * P:(h + 1) * P], keysT[:, j % 2, :],
                                              start=True, stop=True)
                        if j % 4 == 3:
                            mm.then_inc(score_mm, 1)
                project(f"u{layer}", SPLIT)
                pe.wait_ge(chosen_ok, layer + 1)
                for q in range(3):
                    for h in range(HALVES):
                        n = 2 * q + h
                        mm = nc.tensor.transpose(y[:, n // 4, (n % 4) * P:(n % 4 + 1) * P],
                                                 chosen[:, q, h * P:(h + 1) * P], ident[:])
                mm.then_inc(chosen_mm, 1)

                def spread(phase, i, n, q):
                    b = batches_before(layer, phase) + 2 * n + q
                    pe.wait_ge(hots_ok, i * 2 + (b + 1))
                    if n > 0:
                        pe.wait_ge(gated, i * 2 + (b - 1))
                    lo, hi = WIDTHS[phase]
                    banks = spread_banks(phase, q)
                    per_bank = BATCH // banks.shape[1]
                    one = token_parts(onehots[:, q, 0, 0:(hi - lo) * BATCH])
                    for t in range(BATCH):
                        for part in range(2):
                            mm = nc.tensor.matmul(banks[:, t // per_bank, t % per_bank, :],
                                                  token_parts(onehots[:, q, 1 + part, :])[:, t, :],
                                                  one[:, t, :], start=(part == 0), stop=(part == 1))
                    mm.then_inc(spread_ok, 1)

                (_, _, who, offset), = low_parts(FIRST[f"u{layer}"] + SPLIT, end_of[f"u{layer}"])

                def project_round(i, n, c, r):
                    project_block(f"u{layer}", who, offset, i, c)
                    if r == RING - 1:
                        spread(0, i, n, 0)
                        spread(0, i, n, 1)
                in_rounds(pe, FIRST[f"u{layer}"] + SPLIT, ROUNDS, project_round)
                pe.wait_ge(emptied, PROJECTED[f"u{layer}"] + NKEYS)
                pe.wait_ge(gated, batches_before(layer, 1))

                v = f"v{layer}"
                first = FIRST[v]

                def gathered(start, stop, who, offset, i, c):
                    wait_low(who, offset, i, c)
                    pe.wait_ge(a_low, g_of(i, c + 1 - first + NKEYS * layer))
                    combine_block(c % RING, c % RING, start, stop)
                phase_1 = first + RING * ROUNDS
                (_, _, who, offset), = low_parts(first, phase_1)

                def combine_round(i, n, c, r):
                    gathered(c == first, False, who, offset, i, c)
                    if r == RING - 1:
                        spread(1, i, n, 0)
                        spread(1, i, n, 1)
                in_rounds(pe, first, ROUNDS, combine_round)
                for lo, hi, who, offset in low_parts(phase_1, end_of[v]):
                    last = hi == end_of[v]
                    in_threes(pe, lo, hi - last, lambda i, c: gathered(False, False, who, offset, i, c))
                    if last:
                        gathered(False, True, who, offset, 0, hi - 1)
                if layer + 1 < DEPTH:
                    turn_x(2 * layer + 1)

        @block.scalar
        def _(act):
            A = nc.scalar.activation

            def make_high(i, c):
                slot = c % RING
                act.wait_ge(landed[slot], i * 16 + 16 * (c // RING + 1))
                if c >= RING:
                    act.wait_ge(block_used, g_of(i, c - RING + 1))
                A(high[:, slot, :], raw[:, slot, :], ACT.Copy).then_inc(high_made, 1)

            def project(name, empty, first=0):
                g0 = FIRST[name]

                def one(i, c):
                    act.wait_ge(block_used, g_of(i, c + 1))
                    empty(i, c - g0, c % RING)
                    if c + RING < TOTAL:
                        make_high(i, c + RING)
                in_threes(act, g0 + first, end_of[name], one)

            def ln_rows(n):
                for r in range(LN_ROWS[n]):
                    act.dma_start(aux[:, r * D:(r + 1) * D],
                                  ln_par[n, r:r + 1, :].to_broadcast([P, D])).then_inc(ln_in[n], 16)

            def std(n):
                act.wait_ge(var_ok, n + 1)
                A(stats[:, 30:32], stats[:, 28:30], ACT.Sqrt).then_inc(std_ok, 1)

            def split_xT(n):
                for h in range(HALVES):
                    act.wait_ge(x_turned, HALVES * n + h + 1)
                    A(xT_high[:, :, h * P:(h + 1) * P],
                      work[:, 2 * h:2 * h + 2, :].rearrange("p b (k t) -> p (b k) t", t=P),
                      ACT.Copy).then_inc(xT_hi_ok, 1)

            for h in range(HALVES):
                act.dma_start(x[:, h, :], x_rows[h]).then_inc(x_in, 16)
            ln_rows(0)
            act.wait_ge(inputs_in, 16 * 2)
            A(xT_high[:], xT_in.rearrange("p (k t) -> p k t", k=KD), ACT.Copy).then_inc(xT_hi_ok, 1)
            for g in range(RING):
                make_high(0, g)
            act.dma_start(keysT, keys[0]).then_inc(keys_in, 16)

            for t in range(2 * KD):
                act.wait_ge(block_used, t + 1)
                chunk, gate = t // 2, t % 2
                bias = conv_p[:, C_BIN + gate * KD + chunk:C_BIN + gate * KD + chunk + 1]
                if chunk >= 2 and not gate:
                    act.wait_ge(glu_ok, chunk - 1)
                dst = gate_buf if gate else value_buf
                A(dst[:, chunk % 2, :], work[:, t % RING, 0:T], ACT.Sigmoid if gate else ACT.Identity,
                  bias=bias).then_inc(emptied, 1)
                make_high(0, t + RING)
            act.wait_ge(mean_ok, 1)
            A(squares[:], conv[:], ACT.Square).then_inc(sq_ok, 1)
            act.wait_ge(cvar_ok, 1)
            A(std_c, var_c, ACT.Sqrt).then_inc(cstd_ok, 1)
            act.wait_ge(norm_ok, 1)
            for k in range(KD):
                last = A(squares[:, k, :], conv[:, k, :], ACT.Silu,
                         bias=conv_p[:, C_LNB + k:C_LNB + k + 1],
                         scale=conv_p[:, C_LNG + k:C_LNG + k + 1])
            last.then_inc(silu_ok, 1)
            act.wait_ge(silu_ok, 1)
            A(xT_high[:], squares[:], ACT.Copy).then_inc(xT_hi_ok, 1)
            in_threes(act, FIRST["conv_out"], end_of["conv_out"], lambda i, c: make_high(i, c + RING))

            for layer in range(DEPTH):
                if layer == 1:
                    act.wait_ge(block_used, end_of["v0"])
                    for dst, src in ((mla_p, mla_par), (uq_w, w_uq), (uk_w, w_uk), (uv_w, w_uv)):
                        act.dma_start(dst, src).then_inc(mla_in, 16)
                    act.dma_start(keysT, keys[1]).then_inc(keys_in, 16)
                    act.dma_start(pos_i, positions.to_broadcast([P, T])).then_inc(mla_in, 16)
                    act.wait_ge(x_ready, HALVES * 2)
                    ln_rows(2)
                    split_xT(1)

                    def empty(i, t, bank):
                        dst = latent[:, t, :] if t < KQ + KKV else k_rot[:, t - KQ - KKV, :]
                        A(dst, work[:, bank, 0:T], ACT.Copy).then_inc(emptied, 1)
                    g0 = FIRST["mla_in"]
                    for t in range(BLOCKS["mla_in"]):
                        act.wait_ge(block_used, g0 + t + 1)
                        empty(0, t, (g0 + t) % RING)
                        make_high(0, g0 + t + RING)
                    act.wait_ge(emptied, PROJECTED["wq1"])
                    A(lat_sq[:], latent[:], ACT.Square).then_inc(lat_sq_ok, 1)
                    act.wait_ge(rms_var, 1)
                    A(rms[:], rms[:], ACT.Sqrt).then_inc(rms_std, 1)
                    act.wait_ge(ang_ok, 1)
                    A(sinT, angle, ACT.Sin)
                    A(cosT, turns, ACT.Sin).then_inc(trig_ok, 1)
                    for j in range(12 + HEADS):
                        act.wait_ge(small_mm, j + 1)
                        dst = queries[:, j, :] if j < 12 else keys_n[:, j - 12, :]
                        A(dst, work[:, j % 4, 0:T], ACT.Copy).then_inc(small_ok, 1)

                    def exps(h):
                        act.wait_ge(att_m, h + 1)
                        for q in range(HALVES):
                            cols = slice(q * P, q * P + (q + 1) * P)
                            n = 4 * (h % 2) + q
                            mm = A(probs[:, h % 2, cols], probs[:, h % 2, cols], ACT.Exp,
                                   bias=att_st[:, n:n + 1], scale=SCALE,
                                   accum_out=att_st[:, 8 + n:9 + n])
                        mm.then_inc(att_e, 1)

                    def emptyo(h):
                        act.wait_ge(att_o, h + 1)
                        A(xT_high[:, h, :], y[:, h % 2, 0:T],
                          ACT.Copy).then_inc(att_h, 1)
                    exps(0)
                    for h in range(HEADS):
                        if h + 1 < HEADS:
                            exps(h + 1)
                        emptyo(h)
                    in_threes(act, FIRST["mla_out"], end_of["mla_out"],
                              lambda i, c: make_high(i, c + RING))

                std(2 * layer)
                split_xT(2 * layer)
                project(f"wq{layer}", lambda i, t, bank: A(
                    queryT[:, bass.ds(i * RING + t, 1), :].rearrange("p o t -> p (o t)"),
                    work[:, bank, 0:T], ACT.Copy).then_inc(emptied, 1))
                for n in range(HALVES * HP // 4):
                    act.wait_ge(score_mm, 8 * layer + n + 1)
                    A(scores[:, 4 * n:4 * n + 4, :].rearrange("p j n -> p (j n)"), y[:, n % 4, :],
                      ACT.Copy).then_inc(score_ok, 1)

                def gelu(i, t, bank):
                    A(big[:, bass.ds(i * RING + t, 1), :].rearrange("p o t -> p (o t)"),
                      work[:, bank, 0:T], ACT.Gelu).then_inc(emptied, 1)
                u0 = FIRST[f"u{layer}"]
                for part in range(2):
                    a, b = ((u0, u0 + SPLIT), (u0 + SPLIT, u0 + NKEYS))[part]

                    def one(i, c):
                        act.wait_ge(block_used, g_of(i, c + 1))
                        gelu(i, c - u0, c % RING)
                        make_high(i, c + RING)
                    in_threes(act, a, b, one)
                    if part == 0:
                        act.wait_ge(expo_in, layer + 1)
                        A(cand_v, cand_v, ACT.Exp).then_inc(expo_ok, 1)
                        act.wait_ge(chosen_ok, layer + 1)
                v0 = FIRST[f"v{layer}"]
                act.wait_ge(gated, batches_before(layer, 1))

                def a_hi(i, c):
                    A(xT_high[:, c % RING, :],
                      big[:, bass.ds(i * RING + (c - v0), 1), :].rearrange("p o t -> p (o t)"),
                      ACT.Copy).then_inc(a_high, 1)
                for g in range(v0, v0 + RING):
                    a_hi(0, g)

                def one_v(i, c):
                    act.wait_ge(block_used, g_of(i, c + 1))
                    a_hi(i, c + RING)
                    make_high(i, c + RING)
                in_threes(act, v0, v0 + SPLIT - RING, one_v)
                act.wait_ge(gated, batches_before(layer, 2))
                ln_rows(2 * layer + 1)
                in_threes(act, v0 + SPLIT - RING, v0 + NKEYS - RING, one_v)
                if layer + 1 < DEPTH:
                    for g in range(v0 + NKEYS - RING, v0 + NKEYS):
                        make_high(0, g + RING)
                std(2 * layer + 1)

        @block.vector
        def _(dve):
            V = nc.vector
            count = [0]

            def step(ins):
                count[0] += 1
                ins.then_inc(v_step, 1)
                dve.wait_ge(v_step, count[0])

            def low_stage(a, b):
                in_threes(dve, a, b, lambda i, c: make_low(dve, V, "vector", i, c))

            def layer_norm(n):
                dve.wait_ge(ln_in[n], 16 * LN_ROWS[n])
                for h in range(HALVES):
                    xs = x[:, h, :]
                    step(V.scalar_tensor_tensor(xs, xs, ALPHA,
                                                y[:, 2 * h:2 * h + 2, :].rearrange("p b n -> p (b n)"),
                                                ALU.mult, ALU.add))
                    if LN_ROWS[n] == 3:
                        step(V.tensor_tensor(xs, xs, aux[:, 2 * D:3 * D], ALU.add))
                    V.bn_stats(stats[:, 12 * h:12 * h + 6], x[:, h, 0:512])
                    step(V.bn_stats(stats[:, 12 * h + 6:12 * h + 12], x[:, h, 512:1024]))
                    step(V.bn_aggr(stats[:, 24 + 2 * h:26 + 2 * h], stats[:, 12 * h:12 * h + 12]))
                V.tensor_scalar(stats[:, 28:30], stats[:, 25:28:2], LN_EPS, None,
                                ALU.add).then_inc(var_ok, 1)
                dve.wait_ge(std_ok, n + 1)
                step(V.reciprocal(stats[:, 32:34], stats[:, 30:32]))
                for h in range(HALVES):
                    xs = x[:, h, :]
                    step(V.tensor_scalar(xs, xs, stats[:, 24 + 2 * h:25 + 2 * h], stats[:, 32 + h:33 + h],
                                         ALU.subtract, ALU.mult))
                    step(V.tensor_tensor(xs, xs, aux[:, 0:D], ALU.mult))
                    V.tensor_tensor(xs, xs, aux[:, D:2 * D], ALU.add).then_inc(x_ready, 1)

            def split_xT(n, made):
                for h in range(HALVES):
                    dve.wait_ge(xT_hi_ok, made + h + 1)
                    V.tensor_tensor(xT_low[:, :, h * P:(h + 1) * P],
                                    work[:, 2 * h:2 * h + 2, :].rearrange("p b (k t) -> p (b k) t", t=P),
                                    xT_high[:, :, h * P:(h + 1) * P].bitcast(F32),
                                    ALU.subtract).then_inc(xT_lo_ok, 1)

            def select(layer):
                dve.wait_ge(score_ok, 8 * (layer + 1))
                base = layer * (7 * HALVES * HP + 7 * HALVES * PH)

                def top16(i, k0, per):
                    def did(ins, k):
                        ins.then_inc(v_loop, 1)
                        wait_apart(dve, v_loop, i * per + (k0 + k))
                    return did

                with dve.Fori(0, HALVES * HP) as i:
                    did = top16(i, base, 7)
                    ra, rb = row_a[:, 0:NKEYS], row_b[:, 0:NKEYS]
                    did(V.tensor_copy(ra, scores[:, bass.ds(i, 1), :].rearrange("p o n -> p (o n)")), 1)
                    did(V.max(sel_v[:, 0:8], ra), 2)
                    V.max_index(sel_i[:, 0:8], sel_v[:, 0:8], ra)
                    did(V.match_replace(rb, sel_v[:, 0:8], ra, LOWEST), 3)
                    did(V.max(sel_v[:, 8:16], rb), 4)
                    did(V.max_index(sel_i[:, 8:16], sel_v[:, 8:16], rb), 5)
                    did(V.tensor_copy(top_v[:, bass.ds(i * TOPK, TOPK)], sel_v), 6)
                    did(V.tensor_copy(top_i[:, bass.ds(i * TOPK, TOPK)], sel_i), 7)
                base += 7 * HALVES * HP
                with dve.Fori(0, HALVES * PH) as i:
                    did = top16(i, base, 7)
                    did(V.tensor_tensor(row_a.rearrange("p (a b) -> p a b", b=TOPK),
                                        top_v[:, bass.ds(i * 2 * TOPK, TOPK)].unsqueeze(2)
                                        .to_broadcast([P, TOPK, TOPK]),
                                        top_v[:, bass.ds(i * 2 * TOPK + TOPK, TOPK)].unsqueeze(1)
                                        .to_broadcast([P, TOPK, TOPK]), ALU.add), 1)
                    did(V.max(sel_v[:, 0:8], row_a), 2)
                    V.max_index(sel_i[:, 0:8], sel_v[:, 0:8], row_a)
                    did(V.match_replace(row_b, sel_v[:, 0:8], row_a, LOWEST), 3)
                    did(V.max(sel_v[:, 8:16], row_b), 4)
                    did(V.max_index(sel_i[:, 8:16], sel_v[:, 8:16], row_b), 5)
                    did(V.tensor_copy(cand_v[:, bass.ds(i * TOPK, TOPK)], sel_v), 6)
                    did(V.tensor_copy(cand_i[:, bass.ds(i * TOPK, TOPK)], sel_i), 7)
                cv = cand_v.rearrange("p (j k) -> p j k", k=TOPK)
                shape = [P, HALVES * PH, TOPK]
                step(V.tensor_copy(gate_inv, cv[:, :, 0]))
                V.tensor_tensor(cv, cv, gate_inv.unsqueeze(2).to_broadcast(shape),
                                ALU.subtract).then_inc(expo_in, 1)
                V.tensor_scalar(rank1_u, cand_i, 4, None, ALU.logical_shift_right)
                step(V.tensor_scalar(rank2_u, cand_i, TOPK - 1, None, ALU.bitwise_and))
                V.tensor_copy(rank1, rank1_u)
                step(V.tensor_copy(rank2, rank2_u))
                m4 = match.rearrange("p (h k i) -> p h k i", k=TOPK, i=TOPK)
                p4 = picked.rearrange("p (h k i) -> p h k i", k=TOPK, i=TOPK)
                full = [P, PH, TOPK, TOPK]
                for h in range(HALVES):
                    for side, rank in ((0, rank1), (1, rank2)):
                        rk = rank[:, h * P:(h + 1) * P].rearrange("p (h k) -> p h k", k=TOPK)
                        ids = top_i[:, h * HP * TOPK:(h + 1) * HP * TOPK].rearrange(
                            "p (h s i) -> p h s i", s=2, i=TOPK)[:, :, side, :]
                        step(V.tensor_tensor(match.rearrange("p (k i) -> p k i", i=TOPK),
                                             rank[:, h * P:(h + 1) * P].unsqueeze(2)
                                             .to_broadcast([P, P, TOPK]),
                                             iota[:, 0:TOPK].unsqueeze(1).to_broadcast([P, P, TOPK]),
                                             ALU.is_equal))
                        step(V.tensor_tensor(p4, m4, ids.unsqueeze(2).to_broadcast(full), ALU.mult))
                        step(V.tensor_reduce(chosen[:, side, h * P:(h + 1) * P],
                                             picked.rearrange("p (k i) -> p k i", i=TOPK),
                                             AX.X, ALU.add))
                dve.wait_ge(expo_ok, layer + 1)
                step(V.tensor_reduce(gate_sum, cv, AX.X, ALU.add))
                step(V.reciprocal(gate_inv, gate_sum))
                V.tensor_tensor(chosen[:, 2, :].rearrange("p (j k) -> p j k", k=TOPK), cv,
                                gate_inv.unsqueeze(2).to_broadcast(shape),
                                ALU.mult).then_inc(chosen_ok, 1)

            def make_onehots(layer, phase, i, b):
                lo, hi = WIDTHS[phase]

                def equal(dst, q, lo, hi):
                    return V.tensor_tensor(
                        dst.rearrange("p (i t) -> p i t", t=BATCH),
                        iota_b[:, lo * BATCH:hi * BATCH].rearrange("p (i t) -> p i t", t=BATCH),
                        of_tokens(q, hi - lo), ALU.is_equal)

                def of_tokens(q, width):
                    return chosenT[:, q, bass.ds(i * 2 * BATCH + b * BATCH, BATCH)].unsqueeze(
                        1).to_broadcast([P, width, BATCH])
                before = batches_before(layer, phase) + b
                equal(onehots[:, b % 2, 0, 0:(hi - lo) * BATCH], 0, lo, hi)
                if before > 0:
                    dve.wait_ge(hots_ok, i * 2 + before)
                equal(onehot2[:], 1, 0, NKEYS).then_inc(hot2_ok, 1)
                dve.wait_ge(hot2_ok, i * 2 + (before + 1))
                for part in range(2):
                    last = V.tensor_tensor(
                        onehots[:, b % 2, 1 + part, :].rearrange("p (i t) -> p i t", t=BATCH),
                        onehot2[:].rearrange("p (i t) -> p i t", t=BATCH),
                        of_tokens(2 + part, NKEYS), ALU.mult)
                last.then_inc(hots_ok, 1)

            def gate(layer, phase, i, b):
                lo, hi = WIDTHS[phase]
                dve.wait_ge(spread_ok, i * 2 + (batches_before(layer, phase) + b + 1))
                banks = spread_banks(phase, b)
                hid = big[:, lo:hi, bass.ds(i * 2 * BATCH + b * BATCH, BATCH)].rearrange(
                    "p b (u t) -> p u t b", u=banks.shape[1])
                V.scalar_tensor_tensor(hid, banks, 1.0 / GATE_SCALE, hid, ALU.mult,
                                       ALU.mult).then_inc(gated, 1)

            def gate_round(layer, phase, i, n):
                for q in range(2):
                    gate(layer, phase, i, 2 * n + q)
                    if n < ROUNDS - 1:
                        make_onehots(layer, phase, i, 2 * (n + 1) + q)

            def gate_low_blocks(layer):
                dve.wait_ge(chosen_mm, layer + 1)
                V.tensor_copy(chosenT[:].rearrange("p q t -> p (q t)")[:, 0:2 * T], y[:, 0, :])
                scaled = onehot2[:].bitcast(F32)[:, 0:T]
                step(V.tensor_scalar(scaled, y[:, 1, 0:T], GATE_SCALE, None, ALU.mult))
                step(V.tensor_copy(chosenT[:, 2, :], scaled))
                step(V.tensor_tensor(chosenT[:, 3, :], scaled, chosenT[:, 2, :], ALU.subtract))
                for b in range(2):
                    make_onehots(layer, 0, 0, b)
                dve.wait_ge(emptied, PROJECTED[f"u{layer}"] + SPLIT)
                gate_round(layer, 0, 0, 0)
                with dve.Fori(0, ROUNDS - 2) as i:
                    gate_round(layer, 0, i, 1)
                gate_round(layer, 0, 0, ROUNDS - 1)

            def gate_and_combine(layer):
                v0 = FIRST[f"v{layer}"]

                def a_lo(i, c):
                    dve.wait_ge(a_high, g_of(i, c - v0 + NKEYS * layer + 1))
                    V.tensor_tensor(xT_low[:, c % RING, :],
                                    big[:, bass.ds(i * RING + (c - v0), 1), :].rearrange("p o t -> p (o t)"),
                                    xT_high[:, c % RING, :].bitcast(F32),
                                    ALU.subtract).then_inc(a_low, 1)
                for g in range(v0, v0 + RING):
                    a_lo(0, g)
                for b in range(2):
                    make_onehots(layer, 1, 0, b)
                dve.wait_ge(emptied, PROJECTED[f"u{layer}"] + NKEYS)

                def round_(i, n, c, r):
                    a_lo(i, c)
                    if r == RING - 1:
                        gate_round(layer, 1, i, n)
                in_rounds(dve, v0 + RING, ROUNDS, round_)

                def one(i, c):
                    a_lo(i, c)
                    make_low(dve, V, "vector", i, c)
                in_threes(dve, v0 + RING * (ROUNDS + 1), end_of[f"v{layer}"], one)
                if layer + 1 < DEPTH:
                    low_stage(end_of[f"v{layer}"], end_of[f"v{layer}"] + RING)

            dve.wait_ge(consts, 4)
            V.tensor_copy(iota_b[:].rearrange("p (i t) -> p i t", t=BATCH),
                          iota[:].unsqueeze(2).to_broadcast([P, P, BATCH]))
            dve.wait_ge(xT_hi_ok, 1)
            V.tensor_tensor(xT_low[:], xT_in.rearrange("p (k t) -> p k t", k=KD),
                            xT_high[:].bitcast(F32), ALU.subtract).then_inc(xT_lo_ok, 1)
            dve.wait_ge(inputs_in, 32)
            for k in range(KD):
                dve.wait_ge(emptied, 2 * k + 2)
                V.tensor_tensor(padded[:, k, PAD:PAD + T], value_buf[:, k % 2, :], gate_buf[:, k % 2, :],
                                ALU.mult).then_inc(glu_ok, 1)
                dve.wait_ge(glu_ok, k + 1)
                tap = lambda w: conv_p[:, C_TAPS + k * TAPS + w:C_TAPS + k * TAPS + w + 1]
                step(V.tensor_scalar(conv[:, k, :], padded[:, k, 0:T], tap(0),
                                     conv_p[:, C_BDW + k:C_BDW + k + 1], ALU.mult, ALU.add))
                for w in range(1, TAPS):
                    ins = V.scalar_tensor_tensor(conv[:, k, :], padded[:, k, w:w + T], tap(w),
                                                 conv[:, k, :], ALU.mult, ALU.add)
                    if k == KD - 1 and w == TAPS - 1:
                        ins.then_inc(conv_done, 1)
                    else:
                        step(ins)
            over = [P, KD, T]
            dve.wait_ge(stat_mm, 1)
            step(V.tensor_scalar(mean_c, work[:, 3, 0:T], 1.0 / D, None, ALU.mult))
            V.tensor_tensor(conv[:], conv[:], mean_c.unsqueeze(1).to_broadcast(over),
                            ALU.subtract).then_inc(mean_ok, 1)
            dve.wait_ge(stat_mm, 2)
            V.tensor_scalar(var_c, work[:, 3, T:2 * T], 1.0 / D, LN_EPS, ALU.mult,
                            ALU.add).then_inc(cvar_ok, 1)
            dve.wait_ge(cstd_ok, 1)
            step(V.reciprocal(rstd_c, std_c))
            V.tensor_tensor(conv[:], conv[:], rstd_c.unsqueeze(1).to_broadcast(over),
                            ALU.mult).then_inc(norm_ok, 1)
            dve.wait_ge(xT_hi_ok, 2)
            V.tensor_tensor(xT_low[:], squares[:], xT_high[:].bitcast(F32),
                            ALU.subtract).then_inc(xT_lo_ok, 1)
            low_stage(FIRST["conv_out"] + RING, end_of["conv_out"] + RING)
            dve.wait_ge(x_in, 16 * HALVES)
            dve.wait_ge(block_used, end_of["conv_out"])

            for layer in range(DEPTH):
                if layer == 1:
                    split_xT(1, 4)
                    dve.wait_ge(mla_in, 16 * 5)
                    step(V.tensor_copy(angle, pos_i))
                    step(V.tensor_scalar(angle, angle, mla_p[:, M_FREQ:M_FREQ + 1], None, ALU.mult))
                    big_half = 1.5 * 2.0 ** 23
                    step(V.tensor_scalar(turns, angle, 0.15915494309189535, big_half, ALU.mult, ALU.add))
                    step(V.tensor_scalar(turns, turns, big_half, None, ALU.subtract))
                    step(V.tensor_scalar(turns_hi, turns, 1.0 / 4096, big_half, ALU.mult, ALU.add))
                    step(V.tensor_scalar(turns_hi, turns_hi, big_half, 4096.0, ALU.subtract, ALU.mult))
                    step(V.tensor_tensor(turns_lo, turns, turns_hi, ALU.subtract))
                    for part in TWO_PI_PARTS:
                        for k in (turns_hi, turns_lo):
                            step(V.scalar_tensor_tensor(angle, k, -part, angle, ALU.mult, ALU.add))
                    step(V.tensor_scalar(angle, angle, 3.1415925, -3.1415925, ALU.min, ALU.max))
                    step(V.tensor_scalar(spare, angle, -1.0, None, ALU.mult))
                    step(V.tensor_tensor(spare, spare, angle, ALU.max))
                    V.tensor_scalar(turns, spare, -1.0, 1.5707963267948966, ALU.mult,
                                    ALU.add).then_inc(ang_ok, 1)
                    dve.wait_ge(rms_mm, 1)
                    V.tensor_scalar(rms[:, 0, :], work[:, 3, 0:T], 1.0 / Q_RANK, RMS_EPS,
                                    ALU.mult, ALU.add)
                    V.tensor_scalar(rms[:, 1, :], work[:, 3, T:2 * T], 1.0 / KV_RANK, RMS_EPS,
                                    ALU.mult, ALU.add).then_inc(rms_var, 1)
                    dve.wait_ge(rms_std, 1)
                    step(V.reciprocal(rms[:], rms[:]))
                    for k in range(KQ + KKV):
                        last = V.scalar_tensor_tensor(latent_n[:, k, :], latent[:, k, :],
                                                      mla_p[:, k:k + 1], rms[:, int(k >= KQ), :],
                                                      ALU.mult, ALU.mult)
                    last.then_inc(lat_ok, 1)

                    def turn(dst, src, n):
                        for s in range(n):
                            a, b = src[:, 2 * s, :], src[:, 2 * s + 1, :]
                            V.tensor_tensor(turn_tmp[:, 0, :], b, sinT, ALU.mult)
                            V.tensor_tensor(turn_tmp[:, 1, :], a, sinT, ALU.mult)
                            V.tensor_tensor(dst[:, 2 * s, :], a, cosT, ALU.mult)
                            step(V.tensor_tensor(dst[:, 2 * s + 1, :], b, cosT, ALU.mult))
                            V.tensor_tensor(dst[:, 2 * s, :], dst[:, 2 * s, :], turn_tmp[:, 0, :],
                                            ALU.subtract)
                            step(V.tensor_tensor(dst[:, 2 * s + 1, :], dst[:, 2 * s + 1, :],
                                                 turn_tmp[:, 1, :], ALU.add))
                    dve.wait_ge(trig_ok, 1)
                    turn(k_turned, k_rot, 1)
                    dve.wait_ge(consts, 4 + 3)
                    for q in range(4):
                        rows = slice(32 * q, 32 * (q + 1))
                        last = V.tensor_copy(k_masked[rows, q, :, :], k_turned[rows, :, :])
                    step(last)
                    dve.wait_ge(small_ok, 4)
                    turn(q_turned, queries, 2)
                    for h in range(HALVES):
                        dve.wait_ge(value_mm, h + 1)
                        V.tensor_copy(values[:, h, :], y[:, 2 * h:2 * h + 2, :].rearrange("p b n -> p (b n)")
                                      ).then_inc(value_ok, 1)
                    V.memset(att_st[:, 16:17], 0.0).then_inc(q_turn_ok, 1)

                    def maxima(h):
                        dve.wait_ge(att_s, h + 1)
                        if h >= 2:
                            dve.wait_ge(att_t, h - 1)
                        step(V.tensor_tensor(probs[:, h % 2, :], work[:, h % 2, 0:3 * P], mask, ALU.add))
                        n = 4 * (h % 2)
                        V.tensor_reduce(att_st[:, 20:21], probs[:, h % 2, 0:P], AX.X, ALU.max)
                        step(V.tensor_reduce(att_st[:, 21:22], probs[:, h % 2, P:3 * P], AX.X, ALU.max))
                        V.tensor_scalar(att_st[:, n:n + 2], att_st[:, 20:22], -SCALE, None,
                                        ALU.mult).then_inc(att_m, 1)

                    def normalise(h):
                        dve.wait_ge(att_e, h + 1)
                        n = 4 * (h % 2)
                        step(V.reciprocal(att_st[:, 24:26], att_st[:, 8 + n:10 + n]))
                        V.tensor_scalar(probs[:, h % 2, 0:P], probs[:, h % 2, 0:P], att_st[:, 24:25],
                                        None, ALU.mult)
                        V.tensor_scalar(probs[:, h % 2, P:3 * P], probs[:, h % 2, P:3 * P],
                                        att_st[:, 25:26], None, ALU.mult).then_inc(att_p, 1)

                    def copies(h):
                        dve.wait_ge(att_t, h + 1)
                        if h >= 2:
                            dve.wait_ge(att_o, h - 1)
                        V.tensor_copy(probsT[:, h % 2, :], work[:, 2, 0:3 * P]).then_inc(att_c, 1)

                    def out_low(h):
                        dve.wait_ge(att_h, h + 1)
                        V.tensor_tensor(xT_low[:, h, :], y[:, h % 2, 0:T],
                                        xT_high[:, h, :].bitcast(F32), ALU.subtract).then_inc(att_l, 1)
                    maxima(0)
                    for h in range(HEADS):
                        if h + 1 < HEADS:
                            maxima(h + 1)
                        normalise(h)
                        copies(h)
                        if h >= 1:
                            out_low(h - 1)
                    out_low(HEADS - 1)
                    low_stage(FIRST["mla_out"] + RING, end_of["mla_out"] + RING)
                    dve.wait_ge(block_used, end_of["mla_out"])

                layer_norm(2 * layer)
                split_xT(2 * layer, (2, 6)[layer])
                low_stage(FIRST[f"wq{layer}"] + RING, end_of[f"wq{layer}"] + RING)
                select(layer)
                gate_low_blocks(layer)
                gate_and_combine(layer)
                dve.wait_ge(block_used, end_of[f"v{layer}"])
                layer_norm(2 * layer + 1)


def _two_pi_parts():
    import math
    parts, rest = [6.28125], 2 * math.pi - 6.28125
    for _ in range(2):
        scale = 2.0 ** (10 - math.floor(math.log2(rest)))
        parts.append(math.floor(rest * scale) / scale)
        rest -= parts[-1]
    return parts + [rest]


TWO_PI_PARTS = _two_pi_parts()


def kernel(x, positions, conv_w_in, conv_b_in, conv_w_dw, conv_b_dw, conv_ln_g, conv_ln_b,
           conv_w_out, conv_b_out, mla_w_in, mla_q_norm, mla_kv_norm, mla_w_uq, mla_w_uk,
           mla_w_uv, mla_w_out, peer_w_q, peer_sub_keys, peer_u, peer_v,
           ln1_g, ln1_b, ln2_g, ln2_b):
    import numpy as np
    import concourse.bacc as bacc
    from concourse.bass_utils import run_bass_kernel_spmd

    arr = {k: np.asarray(v) for k, v in dict(
        x=x, positions=positions, conv_w_in=conv_w_in, conv_b_in=conv_b_in, conv_w_dw=conv_w_dw,
        conv_b_dw=conv_b_dw, conv_ln_g=conv_ln_g, conv_ln_b=conv_ln_b, conv_w_out=conv_w_out,
        conv_b_out=conv_b_out, mla_w_in=mla_w_in, mla_q_norm=mla_q_norm, mla_kv_norm=mla_kv_norm,
        mla_w_uq=mla_w_uq, mla_w_uk=mla_w_uk, mla_w_uv=mla_w_uv, mla_w_out=mla_w_out,
        peer_w_q=peer_w_q, peer_sub_keys=peer_sub_keys, peer_u=peer_u, peer_v=peer_v,
        ln1_g=ln1_g, ln1_b=ln1_b, ln2_g=ln2_g, ln2_b=ln2_b).items()}

    def stationary(w):
        n = w.shape[1] // P
        return w.reshape(KD, P, n, P).transpose(2, 1, 0, 3).reshape(n, P, KD * P)

    def per_channel(v):
        return v.reshape(-1, P).T

    xr = arr["x"][0]
    w_in = arr["conv_w_in"][0]
    conv_in = stationary(w_in).reshape(2, KD, P, D).transpose(1, 0, 2, 3).reshape(2 * KD, P, D)
    conv_par = np.concatenate(
        [per_channel(arr["conv_b_in"][0]), per_channel(arr["conv_b_dw"][0]),
         per_channel(arr["conv_ln_g"][0]), per_channel(arr["conv_ln_b"][0]),
         arr["conv_w_dw"][0].reshape(TAPS, KD, P).transpose(2, 1, 0).reshape(P, KD * TAPS)], axis=1)

    w = arr["mla_w_in"][0]
    half = ROPE // 2
    r0 = Q_RANK + KV_RANK
    mla_in = stationary(np.concatenate(
        [w[:, :r0], np.tile(w[:, r0:r0 + half], 4), np.tile(w[:, r0 + half:r0 + ROPE], 4)], axis=1))
    uq = arr["mla_w_uq"][0].reshape(Q_RANK, HEADS, NOPE + ROPE)
    rot = [uq[:, 4 * g:4 * g + 4, NOPE + half * s:NOPE + half * (s + 1)].reshape(Q_RANK, P)
           for g in range(2) for s in range(2)]
    uq = np.stack(rot + [uq[:, h, :NOPE] for h in range(HEADS)])
    w_uq = uq.reshape(12, KQ, P, P).transpose(2, 0, 1, 3)
    w_uk = arr["mla_w_uk"][0].reshape(KKV, P, HEADS, P).transpose(1, 2, 0, 3)
    w_uv = arr["mla_w_uv"][0].reshape(KKV, P, D).transpose(1, 0, 2)
    freq = (1.0 / (np.float32(10000.0) ** (np.arange(0, ROPE, 2, dtype=np.float32)
                                           / np.float32(ROPE)))).astype(np.float32)
    mla_par = np.concatenate([per_channel(arr["mla_q_norm"][0]), per_channel(arr["mla_kv_norm"][0]),
                              np.tile(freq, 4)[:, None]], axis=1)

    ln_par = np.stack([np.stack([arr["ln1_g"][0], arr["ln1_b"][0], arr["conv_b_out"][0]]),
                       np.stack([arr["ln2_g"][0], arr["ln2_b"][0], arr["ln2_b"][0]]),
                       np.stack([arr["ln1_g"][1], arr["ln1_b"][1], arr["ln1_b"][1]]),
                       np.stack([arr["ln2_g"][1], arr["ln2_b"][1], arr["ln2_b"][1]])])
    experts = NKEYS * NKEYS
    ins = {
        "x_rows": xr.reshape(HALVES, P, D),
        "x_cols": xr.reshape(T, KD, P).transpose(2, 1, 0),
        "positions": arr["positions"].reshape(1, T),
        "conv_par": conv_par,
        "mla_par": mla_par,
        "ln_par": ln_par,
        "keys": arr["peer_sub_keys"].transpose(0, 3, 1, 2),
        "w_uq": w_uq, "w_uk": w_uk, "w_uv": w_uv,
        "conv_in": conv_in,
        "conv_out": arr["conv_w_out"][0].reshape(KD, P, D),
        "mla_in": mla_in,
        "mla_out": arr["mla_w_out"][0].reshape(KD, P, D),
        "wq": np.stack([stationary(arr["peer_w_q"][n]) for n in range(DEPTH)]),
        "u": arr["peer_u"].reshape(DEPTH, experts // P, P, KD, P).transpose(0, 1, 4, 3, 2)
        .reshape(DEPTH, experts // P, P, KD * P),
        "v": arr["peer_v"].reshape(DEPTH, experts // P, P, D),
    }
    ins = {k: np.ascontiguousarray(v) for k, v in ins.items()}

    nc = bacc.Bacc("TRN2", target_bir_lowering=False, num_devices=1)
    aps = {k: nc.dram_tensor(k, v.shape, mybir.dt.from_np(v.dtype), kind="ExternalInput").ap()
           for k, v in ins.items()}
    out = nc.dram_tensor("out", (HALVES, P, D), F32, kind="ExternalOutput").ap()
    names = ("conv_in", "conv_out", "mla_in", "mla_out", "wq", "u", "v")
    rest = [aps[k] for k in ins if k not in names]
    program(nc, *rest, {k: aps[k] for k in names}, out)
    r = run_bass_kernel_spmd(nc, [ins], core_ids=[0])
    return r.results[0]["out"].reshape(1, T, D)
```

```python
from contextlib import ExitStack

import concourse.bass as bass
from concourse import mybir

F32 = mybir.dt.float32
F32R = mybir.dt.float32r
F16 = mybir.dt.float16
I32 = mybir.dt.int32
U32 = mybir.dt.uint32
ACT = mybir.ActivationFunctionType
ALU = mybir.AluOpType
AX = mybir.AxisListType

P = 128
D = 1024
T = 256
HALVES = T // P
KD = D // P
DEPTH = 2
ALPHA = float((2 * DEPTH) ** 0.25)
LN_EPS = 1e-5
RMS_EPS = 1e-6

TAPS = 31
PAD = TAPS - 1
ROW = PAD + T + 2
PE_CHUNKS = (2, 3, 4)
DVE_CHUNKS = ((0, 1), (5, 6, 7))

HEADS = 8
NOPE, ROPE = 128, 64
Q_RANK, KV_RANK = 384, 256
KQ, KKV = Q_RANK // P, KV_RANK // P
CHUNK = 64
SCALE = float((NOPE + ROPE) ** -0.5)
MASKED = -1e30

PH = 8
NKEYS = 128
TOPK = 16
HP = 2 * PH
LOWEST = -3.0e38

RING = 3
SPLIT = 80
EXP_AT = 66
BATCH = 8
BATCHES = T // BATCH
ROUNDS = BATCHES // 2
WIDTHS = [(0, SPLIT), (SPLIT, NKEYS)]
GATE_SCALE = 2.0 ** 15
assert RING * ROUNDS == NKEYS - SPLIT

DIAGONALS = 4

STREAM = [("conv_in", 2 * KD), ("conv_out", KD), ("wq0", HP), ("u0", NKEYS), ("v0", NKEYS),
          ("mla_in", KQ + KKV + 2), ("mla_out", KD), ("wq1", HP), ("u1", NKEYS), ("v1", NKEYS)]
FIRST, BLOCKS = {}, {}
_g = 0
for _name, _n in STREAM:
    FIRST[_name], BLOCKS[_name] = _g, _n
    _g += _n
TOTAL = _g

LOW_BY = []
_cuts = [(0, "pool"), (FIRST["conv_out"] + RING, "vector")]
for _l in range(DEPTH):
    _cuts += [(FIRST[f"wq{_l}"], "pool"), (FIRST[f"wq{_l}"] + RING, "vector")]
    _cuts += [(FIRST[f"u{_l}"] + RING, "pool"), (FIRST[f"v{_l}"] + RING * (ROUNDS + 1), "vector")]
    if _l == 0:
        _cuts += [(FIRST["mla_in"], "pool")]
_made = {"pool": 0, "vector": 0}
for _i, (_a, _who) in enumerate(_cuts):
    _b = _cuts[_i + 1][0] if _i + 1 < len(_cuts) else TOTAL
    LOW_BY.append((_a, _b, _who, _made[_who]))
    _made[_who] += _b - _a

PROJECTED = {"conv_in": 0, "wq0": 2 * KD, "u0": 2 * KD + HP, "mla_in": 2 * KD + HP + NKEYS}
PROJECTED["wq1"] = PROJECTED["mla_in"] + BLOCKS["mla_in"]
PROJECTED["u1"] = PROJECTED["wq1"] + HP

PARTS = 2
PART = KD // PARTS
SPLITS_BEFORE = [PARTS + KD + HALVES * PARTS * _n for _n in range(2 * DEPTH - 1)]

C_BIN, C_BDW, C_LNG, C_LNB, C_TAPS = 0, 2 * KD, 3 * KD, 4 * KD, 5 * KD
CONV_COLS = 5 * KD + KD * TAPS
M_QN, M_KVN, M_FREQ = 0, KQ, KQ + KKV
MLA_COLS = KQ + KKV + 1
LN_ROWS = [3, 2, 2, 2]


def low_parts(a, b):
    for lo, hi, who, made in LOW_BY:
        if max(a, lo) < min(b, hi):
            yield max(a, lo), min(b, hi), who, made - lo


def in_threes(eng, a, b, body):
    rounds = (b - a) // RING
    if rounds >= 2:
        with eng.Fori(0, rounds) as i:
            for r in range(RING):
                body(i, a + r)
        a += RING * rounds
    for g in range(a, b):
        body(0, g)


def in_rounds(eng, a, rounds, body):
    for r in range(RING):
        body(0, 0, a + r, r)
    with eng.Fori(0, rounds - 2) as i:
        for r in range(RING):
            body(i, 1, a + RING + r, r)
    for r in range(RING):
        body(0, rounds - 1, a + RING * (rounds - 1) + r, r)


def program(nc, x_rows, x_cols, positions, conv_par, mla_par, ln_par, keys, w_uq, w_uk, w_uv,
            blocks, out):
    with ExitStack() as ctx:
        def sb(name, shape, dtype=F32):
            return ctx.enter_context(nc.sbuf_tensor(name, shape, dtype))

        def sem(name):
            return ctx.enter_context(nc.semaphore(name))

        big = sb("big", [P, NKEYS, T])
        raw = sb("raw", [P, RING, D])
        high = sb("high", [P, RING, D], F32R)
        low = sb("low", [P, RING, D], F32R)
        xT_high = sb("xT_high", [P, KD, T], F32R)
        xT_low = sb("xT_low", [P, KD, T], F32R)
        x = sb("x", [P, HALVES, D])
        aux = sb("aux", [P, 3 * D])
        iota = sb("iota", [P, P])
        ident = sb("ident", [P, P])
        ones = sb("ones", [P, P])
        chosenT = sb("chosenT", [P, 4, T], F16)
        iota_b = sb("iota_b", [P, P * BATCH], F16)
        onehot2 = sb("onehot2", [P, P * BATCH], F16)
        warm = sb("warm", [P, 1])
        stats = sb("stats", [P, 64])

        work = ctx.enter_context(nc.psum_tensor("work", [P, 4, 512], F32))
        y = ctx.enter_context(nc.psum_tensor("y", [P, 4, 512], F32))

        def room(slot, width, dtype=None):
            flat = big[:].rearrange("p b t -> p (b t)")[:, slot * T:slot * T + width]
            return flat if dtype is None else flat.bitcast(dtype)

        xT_in = room(0, KD * T).rearrange("p (k t) -> p k t", k=KD)
        conv_p = room(8, CONV_COLS)
        value = room(44, KD * T).rearrange("p (k t) -> p k t", k=KD)
        value_gate = room(52, KD * T).rearrange("p (k t) -> p k t", k=KD)
        padded = room(14, KD * ROW).rearrange("p (k t) -> p k t", k=KD)
        conv = room(24, KD * T).rearrange("p (k t) -> p k t", k=KD)
        squares = room(32, KD * T).rearrange("p (k t) -> p k t", k=KD)
        diagonals = room(60, len(PE_CHUNKS) * TAPS * P).rearrange("p (c w n) -> p c w n", w=TAPS, n=P)
        mean_c, var_c, std_c, rstd_c = (room(40 + n, T) for n in range(4))

        keysT = room(73, 2 * NKEYS).rearrange("p (s n) -> p s n", s=2)
        queryT = room(112, HP * T).rearrange("p (j t) -> p j t", j=HP)
        scores = room(96, HALVES * HP * NKEYS).rearrange("p (j n) -> p j n", n=NKEYS)
        top_v = room(80, HALVES * HP * TOPK)
        top_i = room(82, HALVES * HP * TOPK)
        cand_v = room(84, HALVES * PH * TOPK)
        cand_i = room(85, HALVES * PH * TOPK, U32)
        rank1_u, rank2_u = room(86, T, U32), room(87, T, U32)
        rank1, rank2 = room(88, T), room(89, T)
        sel_v = [room(90, TOPK), room(90, 2 * TOPK)[:, TOPK:]]
        sel_i = [room(91, TOPK, U32), room(91, 2 * TOPK, U32)[:, TOPK:]]
        row_a, row_b = [room(92, T), room(86, T)], [room(93, T), room(87, T)]
        gate_sum = room(94, HALVES * PH)
        gate_inv = room(95, HALVES * PH)
        match = room(96, PH * TOPK * TOPK)
        picked = room(104, PH * TOPK * TOPK)
        onehots = aux[:].bitcast(F16).rearrange("p (s q n) -> p s q n", s=2, q=3)
        chosen = aux[:, 16 * P:16 * P + 3 * T].rearrange("p (q t) -> p q t", q=3)

        latent = room(0, (KQ + KKV) * T).rearrange("p (k t) -> p k t", t=T)
        k_rot = room(5, 2 * T).rearrange("p (s t) -> p s t", s=2)
        lat_sq = room(7, (KQ + KKV) * T).rearrange("p (k t) -> p k t", t=T)
        pos_i = room(12, T, I32)
        angle, turns, turns_hi, turns_lo = (room(13 + n, T) for n in range(4))
        spare = room(17, T)
        cosT, sinT = room(18, T), room(19, T)
        rms = room(20, 2 * T).rearrange("p (s t) -> p s t", s=2)
        latent_n = room(22, (KQ + KKV) * T).rearrange("p (k t) -> p k t", t=T)
        k_turned = room(27, 2 * T).rearrange("p (s t) -> p s t", s=2)
        mla_p = room(29, MLA_COLS)
        mask = room(30, 3 * P)
        queries = room(32, 12 * T).rearrange("p (j t) -> p j t", t=T)
        q_turned = room(44, 4 * T).rearrange("p (j t) -> p j t", t=T)
        turn_tmp = room(48, 2 * T).rearrange("p (s t) -> p s t", s=2)
        keys_n = room(50, HEADS * T).rearrange("p (j t) -> p j t", t=T)
        values = room(58, HALVES * D).rearrange("p (h n) -> p h n", n=D)
        probs = room(66, 2 * 3 * P).rearrange("p (s n) -> p s n", s=2)
        probsT = room(69, 2 * 3 * P).rearrange("p (s n) -> p s n", s=2)
        att_st = room(72, 64)
        uq_w = room(74, 12 * KQ * P).rearrange("p (j k c) -> p j k c", k=KQ, c=P)
        uk_w = room(92, HEADS * KKV * P).rearrange("p (j k c) -> p j k c", k=KKV, c=P)
        uv_w = room(100, KKV * D).rearrange("p (k n) -> p k n", n=D)
        k_masked = room(108, 4 * 2 * T).rearrange("p (q s t) -> p q s t", q=4, s=2)

        landed = [sem(f"block_landed_{s}") for s in range(RING)]
        high_made = sem("high_made")
        low_made = {"pool": sem("low_made_by_pool"), "vector": sem("low_made_by_vector")}
        block_used = sem("block_used")
        emptied = sem("emptied")
        xT_in_ok = [sem(f"xT_input_in_{part}") for part in range(PARTS)]
        conv_par_in = sem("conv_parameters_in")
        keys_in = sem("keys_in")
        x_in = sem("x_in")
        ln_in = [sem(f"ln_rows_in_{n}") for n in range(2 * DEPTH)]
        mla_in = sem("mla_weights_in")
        consts = sem("constants_made")
        pool_fill = sem("pool_fill")
        a_high = sem("a_high_made")
        a_low = sem("a_low_made")
        x_ready = sem("x_normalised")
        x_turned = sem("x_transposed")
        xT_hi_ok = sem("xT_high_made")
        xT_lo_ok = sem("xT_low_made")
        y_half = sem("first_half_combined")
        var_ok = sem("variance_made")
        std_ok = sem("std_made")
        v_step = sem("vector_step")
        v_loop = sem("vector_loop_step")
        a_step = sem("scalar_step")
        glu_ok = sem("glu_made")
        conv_done = sem("conv_done")
        diag_ok = sem("diagonals_made")
        pe_conv = sem("conv_on_tensor_engine")
        pe_conv_ok = sem("conv_on_tensor_engine_copied")
        stat_mm = sem("column_sums_made")
        mean_ok = sem("centred")
        sq_ok = sem("squares_made")
        cvar_ok = sem("conv_variance_made")
        cstd_ok = sem("conv_std_made")
        norm_ok = sem("conv_normalised")
        silu_ok = sem("silu_made")
        score_mm = sem("scores_made")
        score_ok = sem("scores_copied")
        expo_in = sem("gates_centred")
        expo_ok = sem("gates_exponentiated")
        chosen_ok = sem("experts_chosen")
        chosen_mm = sem("chosen_transposed")
        chosenT_ok = sem("chosen_copied")
        hot2_ok = sem("onehot2_made")
        hots_ok = sem("onehots_made")
        spread_ok = sem("gates_spread")
        gated = sem("hidden_gated")
        lat_sq_ok = sem("latent_squares")
        rms_mm = sem("rms_sums")
        rms_var = sem("rms_variance")
        rms_std = sem("rms_std")
        lat_ok = sem("latent_normalised")
        ang_ok = sem("angles_made")
        trig_ok = sem("sines_made")
        small_mm = sem("small_projection")
        small_ok = sem("small_emptied")
        value_mm = sem("values_made")
        value_ok = sem("values_copied")
        q_turn_ok = sem("queries_turned")
        att_s = sem("attention_scores")
        att_m = sem("attention_max")
        att_e = sem("attention_exp")
        att_p = sem("attention_probs")
        att_t = sem("attention_transposed")
        att_c = sem("attention_probsT")
        att_o = sem("attention_out")
        att_h = sem("attention_out_high")
        att_l = sem("attention_out_low")
        out_ok = sem("output_stored")
        waits_taken = sem("waits_taken")

        def g_of(i, c):
            return i * RING + c

        def wait_apart(eng, semaphore, value):
            eng.wait_ge(semaphore, value)
            if not isinstance(value, int):
                eng.sem_inc(waits_taken, 1)

        def batches_before(layer, phase):
            return (2 * layer + phase) * BATCHES

        def token_parts(rows):
            return rows.rearrange("p (i t) -> p t i", t=BATCH)

        def spread_banks(phase, b):
            lo, hi = WIDTHS[phase]
            if phase == 0:
                bank = y[:, 2 * (b % 2):2 * (b % 2) + 2, 0:(hi - lo) * BATCH // 2]
            else:
                bank = work[:, b % 2:b % 2 + 1, 0:(hi - lo) * BATCH]
            return bank.rearrange("p u (t b) -> p u t b", b=hi - lo)

        end_of = {name: FIRST[name] + BLOCKS[name] for name in FIRST}
        block = ctx.enter_context(nc.Block())

        @block.sync
        def _(sp):
            def load(name, i, c):
                slot = c % RING
                src = blocks[name[:-1] if name[-1] in "01" else name]
                at = i * RING + (c - FIRST[name])
                if name[-1] in "01":
                    src = src[int(name[-1])]
                sp.dma_start(raw[:, slot, :],
                             src[bass.ds(at, 1)].rearrange("o p c -> p (o c)")).then_inc(landed[slot], 16)

            for part in range(PARTS):
                ks = slice(PART * part, PART * (part + 1))
                sp.dma_start(xT_in[:, ks, :], x_cols[:, ks, :]).then_inc(xT_in_ok[part], 16)
                if part == 0:
                    load("conv_in", 0, 0)
            sp.dma_start(conv_p, conv_par).then_inc(conv_par_in, 16)
            for g in range(1, RING):
                load("conv_in", 0, g)
            for name, _ in STREAM:
                a = max(FIRST[name], RING)
                for lo, hi, who, offset in low_parts(a - RING, end_of[name] - RING):
                    def one(i, c):
                        wait_apart(sp, high_made, g_of(i, c - RING + 1))
                        wait_apart(sp, low_made[who], g_of(i, c - RING + 1 + offset))
                        load(name, i, c)
                    in_threes(sp, lo + RING, hi + RING, one)
            for h in range(HALVES):
                sp.wait_ge(x_ready, 2 * (2 * DEPTH - 1) + h + 1)
                sp.dma_start(out[h], x[:, h, :]).then_inc(out_ok, 16)
            sp.wait_ge(out_ok, 16 * HALVES)

        def make_low(eng, ops, who, i, c):
            slot = c % RING
            eng.wait_ge(high_made, g_of(i, c + 1))
            ops.tensor_tensor(low[:, slot, :], raw[:, slot, :], high[:, slot, :].bitcast(F32),
                              ALU.subtract).then_inc(low_made[who], 1)

        @block.gpsimd
        def _(pool):
            def low_stage(a, b):
                in_threes(pool, a, b, lambda i, c: make_low(pool, nc.gpsimd, "pool", i, c))

            nc.gpsimd.iota(iota[:], [[1, P]], base=0, channel_multiplier=0,
                           allow_small_or_imprecise_dtypes=True).then_inc(consts, 1)
            nc.gpsimd.memset(ident[:], 0.0).then_inc(pool_fill, 1)
            nc.gpsimd.memset(ones[:], 1.0).then_inc(consts, 1)
            nc.gpsimd.memset(padded[:, :, 0:PAD], 0.0).then_inc(consts, 1)
            pool.wait_ge(pool_fill, 1)
            nc.gpsimd.affine_select(out=ident[:], in_=ident[:], compare_op=ALU.not_equal, fill=1.0,
                                    base=0, pattern=[[-1, P]], channel_multiplier=1).then_inc(consts, 1)
            low_stage(0, FIRST["conv_out"] + RING)
            for layer in range(DEPTH):
                low_stage(FIRST[f"wq{layer}"], FIRST[f"wq{layer}"] + RING)
                low_stage(FIRST[f"u{layer}"] + RING, FIRST[f"v{layer}"] + RING * (ROUNDS + 1))
                if layer == 0:
                    low_stage(FIRST["mla_in"], end_of["mla_in"])
                    nc.gpsimd.memset(mask, 0.0).then_inc(pool_fill, 1)
                    nc.gpsimd.memset(room(108, 4 * 2 * T), 0.0).then_inc(consts, 1)
                    pool.wait_ge(pool_fill, 2)
                    nc.gpsimd.memset(mask[0:CHUNK, CHUNK:P], MASKED).then_inc(consts, 1)
                    nc.gpsimd.memset(mask[0:CHUNK, 3 * P - CHUNK:3 * P], MASKED).then_inc(consts, 1)
                    low_stage(FIRST["mla_out"], end_of["mla_out"])

        @block.tensor
        def _(pe):
            def wait_low(who, offset, i, c):
                pe.wait_ge(low_made[who], g_of(i, c + 1 + offset))

            def project_block(name, who, offset, i, c, splits=None):
                first = FIRST[name]
                wait_low(who, offset, i, c)
                if not (c < first + RING):
                    pe.wait_ge(emptied, g_of(i, c - RING + 1 - first + PROJECTED[name]))
                s = c % RING
                for k in range(KD):
                    if splits is not None and k % PART == 0:
                        wait_xT(splits + k // PART)
                    cols = slice(k * P, (k + 1) * P)
                    for n, (w, m) in enumerate(((high, xT_high), (high, xT_low), (low, xT_high))):
                        mm = nc.tensor.matmul(work[:, s, 0:T], w[:, s, cols], m[:, k, :],
                                              start=(k == 0 and n == 0),
                                              stop=(k == KD - 1 and n == 2))
                mm.then_inc(block_used, 1)

            def project(name, blocks=None, splits=None, skip=0):
                first = FIRST[name]
                for lo, hi, who, offset in low_parts(first + skip, first + (blocks or BLOCKS[name])):
                    def one(i, c):
                        project_block(name, who, offset, i, c)
                    head = min(hi, first + RING)
                    for g in range(lo, head):
                        project_block(name, who, offset, 0, g, splits if g == first else None)
                    in_threes(pe, max(lo, head), hi, one)

            def combine_block(a_slot, s, start, stop, halves=range(HALVES)):
                for h in halves:
                    rows = slice(h * P, (h + 1) * P)
                    for n, (a, v) in enumerate(((xT_high, high), (xT_high, low), (xT_low, high))):
                        for m in range(2):
                            mm = nc.tensor.matmul(y[:, 2 * h + m, :], a[:, a_slot, rows],
                                                  v[:, s, m * 512:(m + 1) * 512],
                                                  start=(start and n == 0), stop=(stop and n == 2))
                if HALVES - 1 in halves:
                    mm.then_inc(block_used, 1)
                return mm

            def combine_last(a_slots, g0, wait_block):
                for h in range(HALVES):
                    for n in range(RING):
                        if h == 0:
                            wait_block(g0 + n)
                        mm = combine_block(a_slots[n], (g0 + n) % RING, False, n == RING - 1, (h,))
                    if h == 0:
                        mm.then_inc(y_half, 1)

            def combine_all(name, wait_chunk):
                last = end_of[name] - RING

                def wait_block(g):
                    for _, _, who, offset in low_parts(g, g + 1):
                        wait_low(who, offset, 0, g)
                    wait_chunk(g - FIRST[name])
                for g in range(FIRST[name], last):
                    wait_block(g)
                    combine_block(g - FIRST[name], g % RING, g == FIRST[name], False)
                combine_last(range(KD - RING, KD), last, wait_block)

            def column_sums(bank, col, src, chunks):
                for n, k in enumerate(chunks):
                    mm = nc.tensor.matmul(work[:, bank, col:col + T], ones[:], src[:, k, :],
                                          start=(n == 0), stop=(n == len(chunks) - 1))
                return mm

            def turn_x(n):
                for h in range(HALVES):
                    pe.wait_ge(x_ready, HALVES * n + h + 1)
                    for k in range(KD):
                        mm = nc.tensor.transpose(work[:, 2 * h + k // 4, (k % 4) * P:(k % 4 + 1) * P],
                                                 x[:, h, k * P:(k + 1) * P], ident[:])
                        if k % PART == PART - 1:
                            mm.then_inc(x_turned, 1)

            def wait_xT(n):
                pe.wait_ge(xT_hi_ok, n)
                pe.wait_ge(xT_lo_ok, n)

            project("conv_in", splits=1)
            pe.wait_ge(consts, 4)
            def chunk_sum(col, src, k, n):
                return nc.tensor.matmul(work[:, 3, col:col + T], ones[:], src[:, k, :],
                                        start=(n == 0), stop=(n == KD - 1))
            for c, k in enumerate(PE_CHUNKS):
                pe.wait_ge(glu_ok, k + 1)
                for w in range(TAPS):
                    pe.wait_ge(diag_ok, c * TAPS + w + 1)
                    mm = nc.tensor.matmul(y[:, c, 0:T], diagonals[:, c, w, :], padded[:, k, w:w + T],
                                          start=(w == 0), stop=(w == TAPS - 1))
                mm.then_inc(pe_conv, 1)
            by_vector = [k for chunks in DVE_CHUNKS for k in chunks]
            order = by_vector[:2] + list(PE_CHUNKS) + by_vector[2:]
            for n, k in enumerate(order):
                if k in PE_CHUNKS:
                    pe.wait_ge(pe_conv_ok, PE_CHUNKS.index(k) + 1)
                else:
                    pe.wait_ge(conv_done, by_vector.index(k) + 1)
                mm = chunk_sum(0, conv, k, n)
            mm.then_inc(stat_mm, 1)
            pe.wait_ge(mean_ok, KD)
            for k in range(KD):
                pe.wait_ge(sq_ok, k + 1)
                mm = chunk_sum(T, squares, k, k)
            mm.then_inc(stat_mm, 1)
            combine_all("conv_out", lambda k: wait_xT(PARTS + k + 1))

            for layer in range(DEPTH):
                if layer == 1:
                    project("mla_in", BLOCKS["mla_in"] - 1,
                            splits=SPLITS_BEFORE[1] + (HALVES - 1) * PARTS + 1)
                    pe.wait_ge(lat_sq_ok, 1)
                    column_sums(3, 0, lat_sq, range(KQ))
                    column_sums(3, T, lat_sq, range(KQ, KQ + KKV)).then_inc(rms_mm, 1)
                    project("mla_in", skip=BLOCKS["mla_in"] - 1)
                    pe.wait_ge(lat_ok, 1)
                    pe.wait_ge(mla_in, 16 * 5)
                    for j in range(12 + HEADS):
                        if j >= 4:
                            pe.wait_ge(small_ok, j - 3)
                        elif j < 3:
                            pe.wait_ge(emptied, PROJECTED["wq1"])
                        if j == 12:
                            pe.wait_ge(lat_ok, 2)
                        w, chunks, k0 = (uq_w[:, j], KQ, 0) if j < 12 else (uk_w[:, j - 12], KKV, KQ)
                        for k in range(chunks):
                            mm = nc.tensor.matmul(work[:, j % 4, 0:T], w[:, k, :], latent_n[:, k0 + k, :],
                                                  start=(k == 0), stop=(k == chunks - 1))
                        mm.then_inc(small_mm, 1)
                    for h in range(HALVES):
                        for m in range(2):
                            for k in range(KKV):
                                mm = nc.tensor.matmul(y[:, 2 * h + m, :],
                                                      latent_n[:, KQ + k, h * P:(h + 1) * P],
                                                      uv_w[:, k, m * 512:(m + 1) * 512],
                                                      start=(k == 0), stop=(k == KKV - 1))
                        mm.then_inc(value_mm, 1)

                    def att_scores(h):
                        if h >= 2:
                            pe.wait_ge(att_m, h - 1)
                        for q in range(HALVES):
                            n = (q + 1) * P
                            cols = slice(q * P, q * P + n)
                            rows = slice(q * P, (q + 1) * P)
                            nc.tensor.matmul(work[:, h % 2, cols], queries[:, 4 + h, rows],
                                             keys_n[:, h, 0:n], start=True, stop=False)
                            for s in range(2):
                                mm = nc.tensor.matmul(work[:, h % 2, cols],
                                                      q_turned[:, 2 * (h // 4) + s, rows],
                                                      k_masked[:, h % 4, s, 0:n],
                                                      start=False, stop=(s == 1))
                        mm.then_inc(att_s, 1)

                    def att_out(h):
                        pe.wait_ge(att_p, h + 1)
                        if h >= 1:
                            pe.wait_ge(att_c, h)
                        for q in range(3):
                            mm = nc.tensor.transpose(work[:, 2, q * P:(q + 1) * P],
                                                     probs[:, h % 2, q * P:(q + 1) * P], ident[:])
                        mm.then_inc(att_t, 1)

                    def att_mix(h):
                        pe.wait_ge(att_c, h + 1)
                        if h >= 1:
                            pe.wait_ge(att_l, h)
                        for q, key, start, stop in ((0, 0, True, True), (1, 0, True, False), (1, 1, False, True)):
                            mm = nc.tensor.matmul(work[:, 3, q * P:(q + 1) * P],
                                                  values[:, key, h * P:(h + 1) * P],
                                                  probsT[:, h % 2, (q + key) * P:(q + key + 1) * P],
                                                  start=start, stop=stop)
                        mm.then_inc(att_o, 1)

                    pe.wait_ge(small_ok, 12 + HEADS)
                    pe.wait_ge(q_turn_ok, 1)
                    pe.wait_ge(value_ok, 2)
                    att_scores(0)
                    att_scores(1)
                    first, last = FIRST["mla_out"], end_of["mla_out"] - RING
                    (_, _, who, offset), = low_parts(first, end_of["mla_out"])
                    for h in range(HEADS):
                        att_out(h)
                        if h + 2 < HEADS:
                            att_scores(h + 2)
                        if 1 <= h and first + h - 1 < last:
                            pe.wait_ge(att_h, h)
                            pe.wait_ge(att_l, h)
                            wait_low(who, offset, 0, first + h - 1)
                            combine_block(h - 1, (first + h - 1) % RING, h == 1, False)
                        att_mix(h)

                    def wait_head(g):
                        pe.wait_ge(att_h, g - first + 1)
                        pe.wait_ge(att_l, g - first + 1)
                        wait_low(who, offset, 0, g)
                    combine_last(range(KD - RING, KD), last, wait_head)

                turn_x(2 * layer)
                project(f"wq{layer}", splits=SPLITS_BEFORE[2 * layer] + (HALVES - 1) * PARTS + 1)
                pe.wait_ge(emptied, PROJECTED[f"wq{layer}"] + HP)
                pe.wait_ge(keys_in, 16 * (layer + 1))
                for h in range(HALVES):
                    for j in range(HP):
                        if j % 4 == 0 and h == 1:
                            pe.wait_ge(score_ok, 8 * layer + j // 4 + 1)
                        mm = nc.tensor.matmul(y[:, j // 4, (j % 4) * P:(j % 4 + 1) * P],
                                              queryT[:, j, h * P:(h + 1) * P], keysT[:, j % 2, :],
                                              start=True, stop=True)
                        if j % 4 == 3:
                            mm.then_inc(score_mm, 1)
                project(f"u{layer}", SPLIT)
                pe.wait_ge(chosen_ok, layer + 1)
                for q in range(3):
                    for h in range(HALVES):
                        n = 2 * q + h
                        mm = nc.tensor.transpose(y[:, n // 4, (n % 4) * P:(n % 4 + 1) * P],
                                                 chosen[:, q, h * P:(h + 1) * P], ident[:])
                mm.then_inc(chosen_mm, 1)

                def spread(phase, i, n, q):
                    b = batches_before(layer, phase) + 2 * n + q
                    pe.wait_ge(hots_ok, i * 2 + (b + 1))
                    if n > 0:
                        pe.wait_ge(gated, i * 2 + (b - 1))
                    lo, hi = WIDTHS[phase]
                    banks = spread_banks(phase, q)
                    per_bank = BATCH // banks.shape[1]
                    one = token_parts(onehots[:, q, 0, 0:(hi - lo) * BATCH])
                    for t in range(BATCH):
                        for part in range(2):
                            mm = nc.tensor.matmul(banks[:, t // per_bank, t % per_bank, :],
                                                  token_parts(onehots[:, q, 1 + part, :])[:, t, :],
                                                  one[:, t, :], start=(part == 0), stop=(part == 1))
                    mm.then_inc(spread_ok, 1)

                (_, _, who, offset), = low_parts(FIRST[f"u{layer}"] + SPLIT, end_of[f"u{layer}"])

                def project_round(i, n, c, r):
                    project_block(f"u{layer}", who, offset, i, c)
                    if r == RING - 1:
                        spread(0, i, n, 0)
                        spread(0, i, n, 1)
                in_rounds(pe, FIRST[f"u{layer}"] + SPLIT, ROUNDS, project_round)
                pe.wait_ge(emptied, PROJECTED[f"u{layer}"] + NKEYS)
                pe.wait_ge(gated, batches_before(layer, 1))

                v = f"v{layer}"
                first = FIRST[v]

                def gathered(start, stop, who, offset, i, c):
                    wait_low(who, offset, i, c)
                    pe.wait_ge(a_low, g_of(i, c + 1 - first + NKEYS * layer))
                    combine_block(c % RING, c % RING, start, stop)
                phase_1 = first + RING * ROUNDS
                (_, _, who, offset), = low_parts(first, phase_1)

                def combine_round(i, n, c, r):
                    gathered(c == first, False, who, offset, i, c)
                    if r == RING - 1:
                        spread(1, i, n, 0)
                        spread(1, i, n, 1)
                in_rounds(pe, first, ROUNDS, combine_round)
                last = end_of[v] - RING
                for lo, hi, who, offset in low_parts(phase_1, end_of[v]):
                    in_threes(pe, lo, min(hi, last), lambda i, c: gathered(False, False, who, offset, i, c))

                def wait_both(g):
                    wait_low(who, offset, 0, g)
                    pe.wait_ge(a_low, g + 1 - FIRST[v] + NKEYS * layer)
                combine_last([g % RING for g in range(last, last + RING)], last, wait_both)
                if layer + 1 < DEPTH:
                    turn_x(2 * layer + 1)

        @block.scalar
        def _(act):
            A = nc.scalar.activation

            def make_high(i, c):
                slot = c % RING
                act.wait_ge(landed[slot], i * 16 + 16 * (c // RING + 1))
                if c >= RING:
                    act.wait_ge(block_used, g_of(i, c - RING + 1))
                A(high[:, slot, :], raw[:, slot, :], ACT.Copy).then_inc(high_made, 1)

            def project(name, empty, first=0):
                g0 = FIRST[name]

                def one(i, c):
                    act.wait_ge(block_used, g_of(i, c + 1))
                    make_high(i, c + RING)
                    empty(i, c - g0, c % RING)
                in_threes(act, g0 + first, end_of[name], one)

            def ln_rows(n):
                for r in range(LN_ROWS[n]):
                    act.dma_start(aux[:, r * D:(r + 1) * D],
                                  ln_par[n, r:r + 1, :].to_broadcast([P, D])).then_inc(ln_in[n], 16)

            def std(n, next_blocks=()):
                A(warm[:], ones[:, 0:1], ACT.Sqrt)
                for h in range(HALVES):
                    if h > 0:
                        for g in next_blocks:
                            make_high(0, g)
                    act.wait_ge(var_ok, HALVES * n + h + 1)
                    A(stats[:, 30 + h:31 + h], stats[:, 28 + h:29 + h], ACT.Sqrt).then_inc(std_ok, 1)

            def split_xT(n):
                for h in range(HALVES):
                    for part in range(PARTS):
                        act.wait_ge(x_turned, PARTS * (HALVES * n + h) + part + 1)
                        A(xT_high[:, PART * part:PART * (part + 1), h * P:(h + 1) * P],
                          work[:, 2 * h + part, :].rearrange("p (k t) -> p k t", t=P),
                          ACT.Copy).then_inc(xT_hi_ok, 1)

            act.wait_ge(xT_in_ok[0], 16)
            for part in range(PARTS):
                if part > 0:
                    make_high(0, 0)
                    act.wait_ge(xT_in_ok[part], 16)
                ks = slice(PART * part, PART * (part + 1))
                A(xT_high[:, ks, :], xT_in[:, ks, :], ACT.Copy).then_inc(xT_hi_ok, 1)
            for g in range(1, RING):
                make_high(0, g)
            act.wait_ge(conv_par_in, 16)
            act.wait_ge(consts, 4)

            def diagonal(n):
                c, w = n // TAPS, n % TAPS
                at = C_TAPS + PE_CHUNKS[c] * TAPS + w
                A(diagonals[:, c, w, :], ident[:], ACT.Identity,
                  scale=conv_p[:, at:at + 1]).then_inc(diag_ok, 1)

            for t in range(2 * KD):
                if t == RING:
                    for h in range(HALVES):
                        act.dma_start(x[:, h, :], x_rows[h]).then_inc(x_in, 16)
                    ln_rows(0)
                act.wait_ge(block_used, t + 1)
                chunk, gate = t // 2, t % 2
                bias = conv_p[:, C_BIN + gate * KD + chunk:C_BIN + gate * KD + chunk + 1]
                dst = value_gate if gate else value
                A(dst[:, chunk, :], work[:, t % RING, 0:T], ACT.Sigmoid if gate else ACT.Identity,
                  bias=bias).then_inc(emptied, 1)
                make_high(0, t + RING)
                for n in range(DIAGONALS * t, DIAGONALS * (t + 1)):
                    diagonal(n)
            for n in range(DIAGONALS * 2 * KD, len(PE_CHUNKS) * TAPS):
                diagonal(n)
            for c, k in enumerate(PE_CHUNKS):
                act.wait_ge(pe_conv, c + 1)
                A(conv[:, k, :], y[:, c, 0:T], ACT.Identity,
                  bias=conv_p[:, C_BDW + k:C_BDW + k + 1]).then_inc(pe_conv_ok, 1)
            act.dma_start(keysT, keys[0]).then_inc(keys_in, 16)
            for k in range(KD):
                act.wait_ge(mean_ok, k + 1)
                A(squares[:, k, :], conv[:, k, :], ACT.Square).then_inc(sq_ok, 1)
            act.wait_ge(cvar_ok, 1)
            A(std_c, var_c, ACT.Sqrt).then_inc(cstd_ok, 1)
            for k in range(KD + 1):
                if k < KD:
                    act.wait_ge(norm_ok, k + 1)
                    A(squares[:, k, :], conv[:, k, :], ACT.Silu,
                      bias=conv_p[:, C_LNB + k:C_LNB + k + 1],
                      scale=conv_p[:, C_LNG + k:C_LNG + k + 1]).then_inc(silu_ok, 1)
                if k > 0:
                    act.wait_ge(silu_ok, k)
                    A(xT_high[:, k - 1, :], squares[:, k - 1, :], ACT.Copy).then_inc(xT_hi_ok, 1)
            in_threes(act, FIRST["conv_out"], end_of["conv_out"] - RING,
                      lambda i, c: make_high(i, c + RING))

            for layer in range(DEPTH):
                if layer == 1:
                    act.wait_ge(block_used, end_of["v0"])
                    for dst, src in ((mla_p, mla_par), (uq_w, w_uq), (uk_w, w_uk), (uv_w, w_uv)):
                        act.dma_start(dst, src).then_inc(mla_in, 16)
                    act.dma_start(keysT, keys[1]).then_inc(keys_in, 16)
                    act.dma_start(pos_i, positions.to_broadcast([P, T])).then_inc(mla_in, 16)
                    act.wait_ge(x_ready, HALVES * 2)
                    ln_rows(2)
                    split_xT(1)

                    def empty(i, t, bank):
                        dst = latent[:, t, :] if t < KQ + KKV else k_rot[:, t - KQ - KKV, :]
                        A(dst, work[:, bank, 0:T], ACT.Copy).then_inc(emptied, 1)
                    g0 = FIRST["mla_in"]
                    for t in range(BLOCKS["mla_in"]):
                        if t == BLOCKS["mla_in"] - 1:
                            A(warm[:], ones[:, 0:1], ACT.Sqrt)
                            act.wait_ge(rms_var, 1)
                            A(rms[:], rms[:], ACT.Sqrt).then_inc(rms_std, 1)
                        act.wait_ge(block_used, g0 + t + 1)
                        empty(0, t, (g0 + t) % RING)
                        if t == KQ + KKV - 1:
                            act.wait_ge(emptied, PROJECTED["mla_in"] + t + 1)
                            A(lat_sq[:], latent[:], ACT.Square).then_inc(lat_sq_ok, 1)
                        make_high(0, g0 + t + RING)
                    act.wait_ge(ang_ok, 1)
                    A(sinT, angle, ACT.Sin)
                    A(cosT, turns, ACT.Sin).then_inc(trig_ok, 1)
                    for j in range(12 + HEADS):
                        act.wait_ge(small_mm, j + 1)
                        dst = queries[:, j, :] if j < 12 else keys_n[:, j - 12, :]
                        A(dst, work[:, j % 4, 0:T], ACT.Copy).then_inc(small_ok, 1)

                    def exps(h):
                        act.wait_ge(att_m, h + 1)
                        for q in range(HALVES):
                            cols = slice(q * P, q * P + (q + 1) * P)
                            n = 4 * (h % 2) + q
                            mm = A(probs[:, h % 2, cols], probs[:, h % 2, cols], ACT.Exp,
                                   bias=att_st[:, n:n + 1], scale=SCALE,
                                   accum_out=att_st[:, 8 + n:9 + n])
                        mm.then_inc(att_e, 1)

                    def emptyo(h):
                        act.wait_ge(att_o, h + 1)
                        A(xT_high[:, h, :], work[:, 3, 0:T],
                          ACT.Copy).then_inc(att_h, 1)
                    exps(0)
                    for h in range(HEADS):
                        if h + 1 < HEADS:
                            exps(h + 1)
                        emptyo(h)
                        if 1 <= h and h - 1 + RING < KD:
                            make_high(0, FIRST["mla_out"] + h - 1 + RING)

                std(2 * layer, range(FIRST[f"wq{layer}"], FIRST[f"wq{layer}"] + RING))
                split_xT(2 * layer)
                project(f"wq{layer}", lambda i, t, bank: A(
                    queryT[:, bass.ds(i * RING + t, 1), :].rearrange("p o t -> p (o t)"),
                    work[:, bank, 0:T], ACT.Copy).then_inc(emptied, 1))
                for n in range(HALVES * HP // 4):
                    act.wait_ge(score_mm, 8 * layer + n + 1)
                    A(scores[:, 4 * n:4 * n + 4, :].rearrange("p j n -> p (j n)"), y[:, n % 4, :],
                      ACT.Copy).then_inc(score_ok, 1)

                def gelu(i, t, bank):
                    A(big[:, bass.ds(i * RING + t, 1), :].rearrange("p o t -> p (o t)"),
                      work[:, bank, 0:T], ACT.Gelu).then_inc(emptied, 1)

                def split_after(i, c):
                    act.wait_ge(block_used, g_of(i, c + 1))
                    make_high(i, c + RING)

                def one(i, c):
                    gelu(i, c - u0, c % RING)
                    split_after(i, c + 1)
                u0 = FIRST[f"u{layer}"]
                split_after(0, u0)
                in_threes(act, u0, u0 + EXP_AT, one)
                act.wait_ge(expo_in, layer + 1)
                A(cand_v, cand_v, ACT.Exp).then_inc(expo_ok, 1)
                in_threes(act, u0 + EXP_AT, u0 + SPLIT - 1, one)
                gelu(0, SPLIT - 1, (u0 + SPLIT - 1) % RING)
                act.wait_ge(chosen_ok, layer + 1)
                split_after(0, u0 + SPLIT)
                in_threes(act, u0 + SPLIT, u0 + NKEYS - 1, one)
                gelu(0, NKEYS - 1, (u0 + NKEYS - 1) % RING)
                v0 = FIRST[f"v{layer}"]
                act.wait_ge(gated, batches_before(layer, 1))

                def a_hi(i, c):
                    A(xT_high[:, c % RING, :],
                      big[:, bass.ds(i * RING + (c - v0), 1), :].rearrange("p o t -> p (o t)"),
                      ACT.Copy).then_inc(a_high, 1)
                for g in range(v0, v0 + RING):
                    a_hi(0, g)

                def one_v(i, c):
                    act.wait_ge(block_used, g_of(i, c + 1))
                    a_hi(i, c + RING)
                    make_high(i, c + RING)
                in_threes(act, v0, v0 + SPLIT - RING, one_v)
                act.wait_ge(gated, batches_before(layer, 2))
                ln_rows(2 * layer + 1)
                in_threes(act, v0 + SPLIT - RING, v0 + NKEYS - RING, one_v)
                std(2 * layer + 1, range(FIRST["mla_in"], FIRST["mla_in"] + RING)
                    if layer + 1 < DEPTH else ())

        @block.vector
        def _(dve):
            V = nc.vector
            count = [0]

            def step(ins):
                count[0] += 1
                ins.then_inc(v_step, 1)
                dve.wait_ge(v_step, count[0])

            def step_before(ins):
                count[0] += 1
                ins.then_inc(v_step, 1)
                if count[0] > 1:
                    dve.wait_ge(v_step, count[0] - 1)

            def low_stage(a, b):
                in_threes(dve, a, b, lambda i, c: make_low(dve, V, "vector", i, c))

            def layer_norm(n, end, bias_in=False):
                dve.wait_ge(ln_in[n], 16 * LN_ROWS[n])
                for h in range(HALVES):
                    xs = x[:, h, :]
                    if h == 0:
                        dve.wait_ge(y_half, n + 1)
                    else:
                        dve.wait_ge(block_used, end)
                    ys = y[:, 2 * h:2 * h + 2, :].rearrange("p b n -> p (b n)")
                    if bias_in:
                        step(V.tensor_tensor(xs, xs, ys, ALU.add))
                    else:
                        step(V.scalar_tensor_tensor(xs, xs, ALPHA, ys, ALU.mult, ALU.add))
                    V.bn_stats(stats[:, 12 * h:12 * h + 6], xs[:, 0:512])
                    step(V.bn_stats(stats[:, 12 * h + 6:12 * h + 12], xs[:, 512:1024]))
                    step(V.bn_aggr(stats[:, 24 + 2 * h:26 + 2 * h], stats[:, 12 * h:12 * h + 12]))
                    V.tensor_scalar(stats[:, 28 + h:29 + h], stats[:, 25 + 2 * h:26 + 2 * h], LN_EPS,
                                    None, ALU.add).then_inc(var_ok, 1)
                    step(V.scalar_tensor_tensor(xs, xs, stats[:, 24 + 2 * h:25 + 2 * h], aux[:, 0:D],
                                                ALU.subtract, ALU.mult))
                    dve.wait_ge(std_ok, HALVES * n + h + 1)
                    step(V.reciprocal(stats[:, 32 + h:33 + h], stats[:, 30 + h:31 + h]))
                    V.scalar_tensor_tensor(xs, xs, stats[:, 32 + h:33 + h], aux[:, D:2 * D],
                                           ALU.mult, ALU.add).then_inc(x_ready, 1)

            def split_xT(n):
                for h in range(HALVES):
                    for part in range(PARTS):
                        dve.wait_ge(xT_hi_ok, SPLITS_BEFORE[n] + PARTS * h + part + 1)
                        at = (slice(None), slice(PART * part, PART * (part + 1)), slice(h * P, (h + 1) * P))
                        V.tensor_tensor(xT_low[at],
                                        work[:, 2 * h + part, :].rearrange("p (k t) -> p k t", t=P),
                                        xT_high[at].bitcast(F32), ALU.subtract).then_inc(xT_lo_ok, 1)

            def select(layer):
                dve.wait_ge(score_ok, 8 * (layer + 1))
                steps = 7
                before = layer * steps * HALVES * (HP + PH)

                def top16(i, before, width, fill, values, indices):
                    def did(ins, k, lane):
                        ins.then_inc(v_loop, 1)
                        n = 2 * k + lane
                        if n > 0:
                            wait_apart(dve, v_loop, i * (2 * steps) + (before + n))
                    for k in range(steps):
                        for lane in range(2):
                            ra, rb = row_a[lane][:, 0:width], row_b[lane][:, 0:width]
                            sv, si = sel_v[lane], sel_i[lane]
                            at = bass.ds(i * 2 * TOPK + lane * TOPK, TOPK)
                            if k == 0:
                                did(fill(ra, i, lane), k, lane)
                            elif k == 1:
                                did(V.max(sv[:, 0:8], ra), k, lane)
                            elif k == 2:
                                V.max_index(si[:, 0:8], sv[:, 0:8], ra)
                                did(V.match_replace(rb, sv[:, 0:8], ra, LOWEST), k, lane)
                            elif k == 3:
                                did(V.max(sv[:, 8:16], rb), k, lane)
                            elif k == 4:
                                did(V.max_index(si[:, 8:16], sv[:, 8:16], rb), k, lane)
                            elif k == 5:
                                did(V.tensor_copy(values[:, at], sv), k, lane)
                            else:
                                did(V.tensor_copy(indices[:, at], si), k, lane)

                def side_scores(ra, i, lane):
                    return V.tensor_copy(
                        ra, scores[:, bass.ds(i * 2 + lane, 1), :].rearrange("p o n -> p (o n)"))

                def sums(ra, i, lane):
                    at = i * 4 * TOPK + lane * 2 * TOPK
                    return V.tensor_tensor(ra.rearrange("p (a b) -> p a b", b=TOPK),
                                           top_v[:, bass.ds(at, TOPK)].unsqueeze(2)
                                           .to_broadcast([P, TOPK, TOPK]),
                                           top_v[:, bass.ds(at + TOPK, TOPK)].unsqueeze(1)
                                           .to_broadcast([P, TOPK, TOPK]), ALU.add)
                with dve.Fori(0, HALVES * HP // 2) as i:
                    top16(i, before, NKEYS, side_scores, top_v, top_i)
                before += steps * HALVES * HP
                dve.wait_ge(v_loop, before)
                with dve.Fori(0, HALVES * PH // 2) as i:
                    top16(i, before, TOPK * TOPK, sums, cand_v, cand_i)
                before += steps * HALVES * PH
                dve.wait_ge(v_loop, before)
                cv = cand_v.rearrange("p (j k) -> p j k", k=TOPK)
                shape = [P, HALVES * PH, TOPK]
                step(V.tensor_copy(gate_inv, cv[:, :, 0]))
                V.tensor_tensor(cv, cv, gate_inv.unsqueeze(2).to_broadcast(shape),
                                ALU.subtract).then_inc(expo_in, 1)
                V.tensor_scalar(rank1_u, cand_i, 4, None, ALU.logical_shift_right)
                step(V.tensor_scalar(rank2_u, cand_i, TOPK - 1, None, ALU.bitwise_and))
                V.tensor_copy(rank1, rank1_u)
                step(V.tensor_copy(rank2, rank2_u))
                m4 = match.rearrange("p (h k i) -> p h k i", k=TOPK, i=TOPK)
                p4 = picked.rearrange("p (h k i) -> p h k i", k=TOPK, i=TOPK)
                full = [P, PH, TOPK, TOPK]
                for h in range(HALVES):
                    for side, rank in ((0, rank1), (1, rank2)):
                        rk = rank[:, h * P:(h + 1) * P].rearrange("p (h k) -> p h k", k=TOPK)
                        ids = top_i[:, h * HP * TOPK:(h + 1) * HP * TOPK].rearrange(
                            "p (h s i) -> p h s i", s=2, i=TOPK)[:, :, side, :]
                        step(V.tensor_tensor(match.rearrange("p (k i) -> p k i", i=TOPK),
                                             rank[:, h * P:(h + 1) * P].unsqueeze(2)
                                             .to_broadcast([P, P, TOPK]),
                                             iota[:, 0:TOPK].unsqueeze(1).to_broadcast([P, P, TOPK]),
                                             ALU.is_equal))
                        step(V.tensor_tensor(p4, m4, ids.unsqueeze(2).to_broadcast(full), ALU.mult))
                        step(V.tensor_reduce(chosen[:, side, h * P:(h + 1) * P],
                                             picked.rearrange("p (k i) -> p k i", i=TOPK),
                                             AX.X, ALU.add))
                dve.wait_ge(expo_ok, layer + 1)
                step(V.tensor_reduce(gate_sum, cv, AX.X, ALU.add))
                step(V.reciprocal(gate_inv, gate_sum))
                V.tensor_tensor(chosen[:, 2, :].rearrange("p (j k) -> p j k", k=TOPK), cv,
                                gate_inv.unsqueeze(2).to_broadcast(shape),
                                ALU.mult).then_inc(chosen_ok, 1)

            def make_onehots(layer, phase, i, b):
                lo, hi = WIDTHS[phase]

                def equal(dst, q, lo, hi):
                    return V.tensor_tensor(
                        dst.rearrange("p (i t) -> p i t", t=BATCH),
                        iota_b[:, lo * BATCH:hi * BATCH].rearrange("p (i t) -> p i t", t=BATCH),
                        of_tokens(q, hi - lo), ALU.is_equal)

                def of_tokens(q, width):
                    return chosenT[:, q, bass.ds(i * 2 * BATCH + b * BATCH, BATCH)].unsqueeze(
                        1).to_broadcast([P, width, BATCH])
                before = batches_before(layer, phase) + b
                equal(onehots[:, b % 2, 0, 0:(hi - lo) * BATCH], 0, lo, hi)
                if before > 0:
                    dve.wait_ge(hots_ok, i * 2 + before)
                equal(onehot2[:], 1, 0, NKEYS).then_inc(hot2_ok, 1)
                dve.wait_ge(hot2_ok, i * 2 + (before + 1))
                for part in range(2):
                    last = V.tensor_tensor(
                        onehots[:, b % 2, 1 + part, :].rearrange("p (i t) -> p i t", t=BATCH),
                        onehot2[:].rearrange("p (i t) -> p i t", t=BATCH),
                        of_tokens(2 + part, NKEYS), ALU.mult)
                last.then_inc(hots_ok, 1)

            def gate(layer, phase, i, b):
                lo, hi = WIDTHS[phase]
                dve.wait_ge(spread_ok, i * 2 + (batches_before(layer, phase) + b + 1))
                banks = spread_banks(phase, b)
                hid = big[:, lo:hi, bass.ds(i * 2 * BATCH + b * BATCH, BATCH)].rearrange(
                    "p b (u t) -> p u t b", u=banks.shape[1])
                V.scalar_tensor_tensor(hid, banks, 1.0 / GATE_SCALE, hid, ALU.mult,
                                       ALU.mult).then_inc(gated, 1)

            def gate_round(layer, phase, i, n):
                for q in range(2):
                    gate(layer, phase, i, 2 * n + q)
                    if n < ROUNDS - 1:
                        make_onehots(layer, phase, i, 2 * (n + 1) + q)

            def gate_low_blocks(layer):
                dve.wait_ge(chosen_mm, layer + 1)
                V.tensor_copy(chosenT[:].rearrange("p q t -> p (q t)")[:, 0:2 * T], y[:, 0, :])
                scaled = onehot2[:].bitcast(F32)[:, 0:T]
                step(V.tensor_scalar(scaled, y[:, 1, 0:T], GATE_SCALE, None, ALU.mult))
                step(V.tensor_copy(chosenT[:, 2, :], scaled))
                step(V.tensor_tensor(chosenT[:, 3, :], scaled, chosenT[:, 2, :], ALU.subtract))
                for b in range(2):
                    make_onehots(layer, 0, 0, b)
                dve.wait_ge(emptied, PROJECTED[f"u{layer}"] + SPLIT)
                gate_round(layer, 0, 0, 0)
                with dve.Fori(0, ROUNDS - 2) as i:
                    gate_round(layer, 0, i, 1)
                gate_round(layer, 0, 0, ROUNDS - 1)

            def gate_and_combine(layer):
                v0 = FIRST[f"v{layer}"]

                def a_lo(i, c):
                    dve.wait_ge(a_high, g_of(i, c - v0 + NKEYS * layer + 1))
                    V.tensor_tensor(xT_low[:, c % RING, :],
                                    big[:, bass.ds(i * RING + (c - v0), 1), :].rearrange("p o t -> p (o t)"),
                                    xT_high[:, c % RING, :].bitcast(F32),
                                    ALU.subtract).then_inc(a_low, 1)
                for g in range(v0, v0 + RING):
                    a_lo(0, g)
                for b in range(2):
                    make_onehots(layer, 1, 0, b)
                dve.wait_ge(emptied, PROJECTED[f"u{layer}"] + NKEYS)

                def round_(i, n, c, r):
                    a_lo(i, c)
                    if r == RING - 1:
                        gate_round(layer, 1, i, n)
                in_rounds(dve, v0 + RING, ROUNDS, round_)

                def one(i, c):
                    a_lo(i, c)
                    make_low(dve, V, "vector", i, c)
                in_threes(dve, v0 + RING * (ROUNDS + 1), end_of[f"v{layer}"], one)

            for part in range(PARTS):
                ks = slice(PART * part, PART * (part + 1))
                dve.wait_ge(xT_hi_ok, part + 1)
                V.tensor_tensor(xT_low[:, ks, :], xT_in[:, ks, :], xT_high[:, ks, :].bitcast(F32),
                                ALU.subtract).then_inc(xT_lo_ok, 1)
            dve.wait_ge(consts, 4)
            V.tensor_copy(iota_b[:].rearrange("p (i t) -> p i t", t=BATCH),
                          iota[:].unsqueeze(2).to_broadcast([P, P, BATCH]))
            dve.wait_ge(conv_par_in, 16)
            tap = lambda k, w: conv_p[:, C_TAPS + k * TAPS + w:C_TAPS + k * TAPS + w + 1]
            def glu(k):
                dve.wait_ge(emptied, 2 * k + 2)
                V.tensor_tensor(padded[:, k, PAD:PAD + T], value[:, k, :], value_gate[:, k, :],
                                ALU.mult).then_inc(glu_ok, 1)
            for chunks in DVE_CHUNKS:
                for k in chunks:
                    glu(k)
                for w in range(TAPS):
                    if chunks == DVE_CHUNKS[0] and w == TAPS - 5:
                        for k in PE_CHUNKS:
                            glu(k)
                    for k in chunks:
                        if w == TAPS - 1:
                            dve.wait_ge(v_step, count[0])
                        if w == 0:
                            dve.wait_ge(glu_ok, k + 1)
                            ins = V.tensor_scalar(conv[:, k, :], padded[:, k, 0:T], tap(k, 0),
                                                  conv_p[:, C_BDW + k:C_BDW + k + 1],
                                                  ALU.mult, ALU.add)
                        else:
                            ins = V.scalar_tensor_tensor(conv[:, k, :], padded[:, k, w:w + T],
                                                         tap(k, w), conv[:, k, :],
                                                         ALU.mult, ALU.add)
                        if w < TAPS - 1:
                            step_before(ins)
                        else:
                            ins.then_inc(conv_done, 1)
            dve.wait_ge(pe_conv_ok, len(PE_CHUNKS))
            dve.wait_ge(stat_mm, 1)
            step(V.tensor_scalar(mean_c, work[:, 3, 0:T], 1.0 / D, None, ALU.mult))
            for k in range(KD):
                V.tensor_tensor(conv[:, k, :], conv[:, k, :], mean_c, ALU.subtract).then_inc(mean_ok, 1)
            dve.wait_ge(stat_mm, 2)
            V.tensor_scalar(var_c, work[:, 3, T:2 * T], 1.0 / D, LN_EPS, ALU.mult,
                            ALU.add).then_inc(cvar_ok, 1)
            dve.wait_ge(cstd_ok, 1)
            step(V.reciprocal(rstd_c, std_c))
            for k in range(KD + 2):
                if k < KD:
                    V.tensor_tensor(conv[:, k, :], conv[:, k, :], rstd_c, ALU.mult).then_inc(norm_ok, 1)
                if k >= 2:
                    dve.wait_ge(xT_hi_ok, PARTS + k - 1)
                    V.tensor_tensor(xT_low[:, k - 2, :], squares[:, k - 2, :],
                                    xT_high[:, k - 2, :].bitcast(F32),
                                    ALU.subtract).then_inc(xT_lo_ok, 1)
            dve.wait_ge(x_in, 16 * HALVES)
            dve.wait_ge(ln_in[0], 16 * LN_ROWS[0])
            for h in range(HALVES):
                last = V.scalar_tensor_tensor(x[:, h, :], x[:, h, :], ALPHA, aux[:, 2 * D:3 * D],
                                              ALU.mult, ALU.add)
            step(last)
            low_stage(FIRST["conv_out"] + RING, end_of["conv_out"])

            for layer in range(DEPTH):
                if layer == 1:
                    split_xT(1)
                    dve.wait_ge(mla_in, 16 * 5)
                    step(V.tensor_copy(angle, pos_i))
                    step(V.tensor_scalar(angle, angle, mla_p[:, M_FREQ:M_FREQ + 1], None, ALU.mult))
                    big_half = 1.5 * 2.0 ** 23
                    step(V.tensor_scalar(turns, angle, 0.15915494309189535, big_half, ALU.mult, ALU.add))
                    step(V.tensor_scalar(turns, turns, big_half, None, ALU.subtract))
                    step(V.tensor_scalar(turns_hi, turns, 1.0 / 4096, big_half, ALU.mult, ALU.add))
                    step(V.tensor_scalar(turns_hi, turns_hi, big_half, 4096.0, ALU.subtract, ALU.mult))
                    step(V.tensor_tensor(turns_lo, turns, turns_hi, ALU.subtract))
                    for part in TWO_PI_PARTS:
                        for k in (turns_hi, turns_lo):
                            step(V.scalar_tensor_tensor(angle, k, -part, angle, ALU.mult, ALU.add))
                    step(V.tensor_scalar(angle, angle, 3.1415925, -3.1415925, ALU.min, ALU.max))
                    step(V.tensor_scalar(spare, angle, -1.0, None, ALU.mult))
                    step(V.tensor_tensor(spare, spare, angle, ALU.max))
                    V.tensor_scalar(turns, spare, -1.0, 1.5707963267948966, ALU.mult,
                                    ALU.add).then_inc(ang_ok, 1)
                    dve.wait_ge(rms_mm, 1)
                    V.tensor_scalar(rms[:, 0, :], work[:, 3, 0:T], 1.0 / Q_RANK, RMS_EPS,
                                    ALU.mult, ALU.add)
                    V.tensor_scalar(rms[:, 1, :], work[:, 3, T:2 * T], 1.0 / KV_RANK, RMS_EPS,
                                    ALU.mult, ALU.add).then_inc(rms_var, 1)
                    dve.wait_ge(rms_std, 1)
                    for part, ks in ((0, range(KQ)), (1, range(KQ, KQ + KKV))):
                        step(V.reciprocal(rms[:, part, :], rms[:, part, :]))
                        for k in ks:
                            last = V.scalar_tensor_tensor(latent_n[:, k, :], latent[:, k, :],
                                                          mla_p[:, k:k + 1], rms[:, part, :],
                                                          ALU.mult, ALU.mult)
                        last.then_inc(lat_ok, 1)

                    def turn(dst, src, n):
                        for s in range(n):
                            a, b = src[:, 2 * s, :], src[:, 2 * s + 1, :]
                            V.tensor_tensor(turn_tmp[:, 0, :], b, sinT, ALU.mult)
                            V.tensor_tensor(turn_tmp[:, 1, :], a, sinT, ALU.mult)
                            V.tensor_tensor(dst[:, 2 * s, :], a, cosT, ALU.mult)
                            step(V.tensor_tensor(dst[:, 2 * s + 1, :], b, cosT, ALU.mult))
                            V.tensor_tensor(dst[:, 2 * s, :], dst[:, 2 * s, :], turn_tmp[:, 0, :],
                                            ALU.subtract)
                            step(V.tensor_tensor(dst[:, 2 * s + 1, :], dst[:, 2 * s + 1, :],
                                                 turn_tmp[:, 1, :], ALU.add))
                    dve.wait_ge(trig_ok, 1)
                    turn(k_turned, k_rot, 1)
                    dve.wait_ge(consts, 4 + 3)
                    for q in range(4):
                        rows = slice(32 * q, 32 * (q + 1))
                        last = V.tensor_copy(k_masked[rows, q, :, :], k_turned[rows, :, :])
                    step(last)
                    dve.wait_ge(small_ok, 4)
                    turn(q_turned, queries, 2)
                    for h in range(HALVES):
                        dve.wait_ge(value_mm, h + 1)
                        V.tensor_copy(values[:, h, :], y[:, 2 * h:2 * h + 2, :].rearrange("p b n -> p (b n)")
                                      ).then_inc(value_ok, 1)
                    V.memset(att_st[:, 16:17], 0.0).then_inc(q_turn_ok, 1)

                    def maxima(h):
                        dve.wait_ge(att_s, h + 1)
                        if h >= 2:
                            dve.wait_ge(att_t, h - 1)
                        step(V.tensor_tensor(probs[:, h % 2, :], work[:, h % 2, 0:3 * P], mask, ALU.add))
                        n = 4 * (h % 2)
                        V.tensor_reduce(att_st[:, 20:21], probs[:, h % 2, 0:P], AX.X, ALU.max)
                        step(V.tensor_reduce(att_st[:, 21:22], probs[:, h % 2, P:3 * P], AX.X, ALU.max))
                        V.tensor_scalar(att_st[:, n:n + 2], att_st[:, 20:22], -SCALE, None,
                                        ALU.mult).then_inc(att_m, 1)

                    def normalise(h):
                        dve.wait_ge(att_e, h + 1)
                        n = 4 * (h % 2)
                        step(V.reciprocal(att_st[:, 24:26], att_st[:, 8 + n:10 + n]))
                        V.tensor_scalar(probs[:, h % 2, 0:P], probs[:, h % 2, 0:P], att_st[:, 24:25],
                                        None, ALU.mult)
                        V.tensor_scalar(probs[:, h % 2, P:3 * P], probs[:, h % 2, P:3 * P],
                                        att_st[:, 25:26], None, ALU.mult).then_inc(att_p, 1)

                    def copies(h):
                        dve.wait_ge(att_t, h + 1)
                        if h >= 2:
                            dve.wait_ge(att_o, h - 1)
                        V.tensor_copy(probsT[:, h % 2, :], work[:, 2, 0:3 * P]).then_inc(att_c, 1)

                    def out_low(h):
                        dve.wait_ge(att_h, h + 1)
                        V.tensor_tensor(xT_low[:, h, :], work[:, 3, 0:T],
                                        xT_high[:, h, :].bitcast(F32), ALU.subtract).then_inc(att_l, 1)
                    maxima(0)
                    for h in range(HEADS):
                        if h + 1 < HEADS:
                            maxima(h + 1)
                        normalise(h)
                        copies(h)
                        if h >= 1:
                            out_low(h - 1)
                    out_low(HEADS - 1)

                layer_norm(2 * layer, end_of[("conv_out", "mla_out")[layer]], bias_in=(layer == 0))
                split_xT(2 * layer)
                low_stage(FIRST[f"wq{layer}"] + RING, end_of[f"wq{layer}"] + RING)
                select(layer)
                gate_low_blocks(layer)
                gate_and_combine(layer)
                layer_norm(2 * layer + 1, end_of[f"v{layer}"])


def _two_pi_parts():
    import math
    parts, rest = [6.28125], 2 * math.pi - 6.28125
    for _ in range(2):
        scale = 2.0 ** (10 - math.floor(math.log2(rest)))
        parts.append(math.floor(rest * scale) / scale)
        rest -= parts[-1]
    return parts + [rest]


TWO_PI_PARTS = _two_pi_parts()


def kernel(x, positions, conv_w_in, conv_b_in, conv_w_dw, conv_b_dw, conv_ln_g, conv_ln_b,
           conv_w_out, conv_b_out, mla_w_in, mla_q_norm, mla_kv_norm, mla_w_uq, mla_w_uk,
           mla_w_uv, mla_w_out, peer_w_q, peer_sub_keys, peer_u, peer_v,
           ln1_g, ln1_b, ln2_g, ln2_b):
    import numpy as np
    import concourse.bacc as bacc
    from concourse.bass_utils import run_bass_kernel_spmd

    arr = {k: np.asarray(v) for k, v in dict(
        x=x, positions=positions, conv_w_in=conv_w_in, conv_b_in=conv_b_in, conv_w_dw=conv_w_dw,
        conv_b_dw=conv_b_dw, conv_ln_g=conv_ln_g, conv_ln_b=conv_ln_b, conv_w_out=conv_w_out,
        conv_b_out=conv_b_out, mla_w_in=mla_w_in, mla_q_norm=mla_q_norm, mla_kv_norm=mla_kv_norm,
        mla_w_uq=mla_w_uq, mla_w_uk=mla_w_uk, mla_w_uv=mla_w_uv, mla_w_out=mla_w_out,
        peer_w_q=peer_w_q, peer_sub_keys=peer_sub_keys, peer_u=peer_u, peer_v=peer_v,
        ln1_g=ln1_g, ln1_b=ln1_b, ln2_g=ln2_g, ln2_b=ln2_b).items()}

    def stationary(w):
        n = w.shape[1] // P
        return w.reshape(KD, P, n, P).transpose(2, 1, 0, 3).reshape(n, P, KD * P)

    def per_channel(v):
        return v.reshape(-1, P).T

    xr = arr["x"][0]
    w_in = arr["conv_w_in"][0]
    conv_in = stationary(w_in).reshape(2, KD, P, D).transpose(1, 0, 2, 3).reshape(2 * KD, P, D)
    conv_par = np.concatenate(
        [per_channel(arr["conv_b_in"][0]), per_channel(arr["conv_b_dw"][0]),
         per_channel(arr["conv_ln_g"][0]), per_channel(arr["conv_ln_b"][0]),
         arr["conv_w_dw"][0].reshape(TAPS, KD, P).transpose(2, 1, 0).reshape(P, KD * TAPS)], axis=1)

    w = arr["mla_w_in"][0]
    half = ROPE // 2
    r0 = Q_RANK + KV_RANK
    mla_in = stationary(np.concatenate(
        [w[:, :r0], np.tile(w[:, r0:r0 + half], 4), np.tile(w[:, r0 + half:r0 + ROPE], 4)], axis=1))
    uq = arr["mla_w_uq"][0].reshape(Q_RANK, HEADS, NOPE + ROPE)
    rot = [uq[:, 4 * g:4 * g + 4, NOPE + half * s:NOPE + half * (s + 1)].reshape(Q_RANK, P)
           for g in range(2) for s in range(2)]
    uq = np.stack(rot + [uq[:, h, :NOPE] for h in range(HEADS)])
    w_uq = uq.reshape(12, KQ, P, P).transpose(2, 0, 1, 3)
    w_uk = arr["mla_w_uk"][0].reshape(KKV, P, HEADS, P).transpose(1, 2, 0, 3)
    w_uv = arr["mla_w_uv"][0].reshape(KKV, P, D).transpose(1, 0, 2)
    freq = (1.0 / (np.float32(10000.0) ** (np.arange(0, ROPE, 2, dtype=np.float32)
                                           / np.float32(ROPE)))).astype(np.float32)
    mla_par = np.concatenate([per_channel(arr["mla_q_norm"][0]), per_channel(arr["mla_kv_norm"][0]),
                              np.tile(freq, 4)[:, None]], axis=1)

    ln_par = np.stack([np.stack([arr["ln1_g"][0], arr["ln1_b"][0], arr["conv_b_out"][0]]),
                       np.stack([arr["ln2_g"][0], arr["ln2_b"][0], arr["ln2_b"][0]]),
                       np.stack([arr["ln1_g"][1], arr["ln1_b"][1], arr["ln1_b"][1]]),
                       np.stack([arr["ln2_g"][1], arr["ln2_b"][1], arr["ln2_b"][1]])])
    experts = NKEYS * NKEYS
    ins = {
        "x_rows": xr.reshape(HALVES, P, D),
        "x_cols": xr.reshape(T, KD, P).transpose(2, 1, 0),
        "positions": arr["positions"].reshape(1, T),
        "conv_par": conv_par,
        "mla_par": mla_par,
        "ln_par": ln_par,
        "keys": arr["peer_sub_keys"].transpose(0, 3, 1, 2),
        "w_uq": w_uq, "w_uk": w_uk, "w_uv": w_uv,
        "conv_in": conv_in,
        "conv_out": arr["conv_w_out"][0].reshape(KD, P, D),
        "mla_in": mla_in,
        "mla_out": arr["mla_w_out"][0].reshape(KD, P, D),
        "wq": np.stack([stationary(arr["peer_w_q"][n]) for n in range(DEPTH)]),
        "u": arr["peer_u"].reshape(DEPTH, experts // P, P, KD, P).transpose(0, 1, 4, 3, 2)
        .reshape(DEPTH, experts // P, P, KD * P),
        "v": arr["peer_v"].reshape(DEPTH, experts // P, P, D),
    }
    ins = {k: np.ascontiguousarray(v) for k, v in ins.items()}

    nc = bacc.Bacc("TRN2", target_bir_lowering=False, num_devices=1)
    aps = {k: nc.dram_tensor(k, v.shape, mybir.dt.from_np(v.dtype), kind="ExternalInput").ap()
           for k, v in ins.items()}
    out = nc.dram_tensor("out", (HALVES, P, D), F32, kind="ExternalOutput").ap()
    names = ("conv_in", "conv_out", "mla_in", "mla_out", "wq", "u", "v")
    rest = [aps[k] for k in ins if k not in names]
    program(nc, *rest, {k: aps[k] for k in names}, out)
    r = run_bass_kernel_spmd(nc, [ins], core_ids=[0])
    return r.results[0]["out"].reshape(1, T, D)
```
